# Optimizing a Trainium2 kernel written in Bass

```python
import math
import jax, jax.numpy as jnp
from jax import lax
import numpy as np

D_MODEL = 1024
BATCH = 1
SEQ = 512
DEPTH = 1
DEC_BATCH = 8
DEC_SEQ = 4
PAST_LEN = 1024
PAGE_SIZE = 128

D_MIX = D_MODEL
D_A = D_MIX // 4
G_A = 4
GD_A = D_A // G_A
CHUNK = 128
HEAD_DIM = 64
H_B = (D_MIX - D_A) // HEAD_DIM
D_B = H_B * HEAD_DIM
D_IN = 2 * D_A + 3 * D_B
DILATED = ((128, 1), (512, 4), (2048, 16))
WIN_MAX = max(w for w, _ in DILATED)
QBLK = 128
ROT_DIM = HEAD_DIM // 4
ROPE_THETA = 500000.0
PEER_HEADS = 8
N_KEYS = 128
N_EXPERTS = N_KEYS * N_KEYS
D_KEY = 256
DK_HALF = D_KEY // 2
TOPK = 16
TOK_BLK = 256
EPS = 1e-6
NEG = -1e30

kernel_name = "hybrid_gmlp_dilated_peer_step"

def rmsnorm(x, g):
    xf = x.astype(jnp.float32)
    y = xf * lax.rsqrt(jnp.mean(xf * xf, axis=-1, keepdims=True) + EPS)
    return y.astype(x.dtype) * g

def layernorm(x, g, b):
    xf = x.astype(jnp.float32)
    mu = jnp.mean(xf, axis=-1, keepdims=True)
    var = jnp.mean(jnp.square(xf - mu), axis=-1, keepdims=True)
    y = (xf - mu) * lax.rsqrt(var + EPS)
    return y.astype(x.dtype) * g + b

def rope_partial(x, pos):
    inv = ROPE_THETA ** (-jnp.arange(0, ROT_DIM, 2, dtype=jnp.float32) / ROT_DIM)
    ang = pos.astype(jnp.float32)[:, None] * inv[None, :]
    cos = jnp.cos(ang)[:, None, :]
    sin = jnp.sin(ang)[:, None, :]
    xr = x[..., :ROT_DIM].astype(jnp.float32)
    x1, x2 = xr[..., :ROT_DIM // 2], xr[..., ROT_DIM // 2:]
    rot = jnp.concatenate([x1 * cos - x2 * sin, x2 * cos + x1 * sin], axis=-1)
    return jnp.concatenate([rot.astype(x.dtype), x[..., ROT_DIM:]], axis=-1)

def mix_projection(h, w_in, ln_g, ln_b, pos):
    proj = h @ w_in
    lead = proj.shape[:-1]
    u = proj[..., :D_A]
    vn = layernorm(proj[..., D_A:2 * D_A], ln_g, ln_b)
    o = 2 * D_A
    q = proj[..., o:o + D_B].reshape(lead + (H_B, HEAD_DIM))
    k = proj[..., o + D_B:o + 2 * D_B].reshape(lead + (H_B, HEAD_DIM))
    v = proj[..., o + 2 * D_B:o + 3 * D_B].reshape(lead + (H_B, HEAD_DIM))
    q = rope_partial(q, pos) * (HEAD_DIM ** -0.5)
    k = rope_partial(k, pos)
    return u, vn, q, k, v

def gmlp_chunk_prompt(u, vn, w_s, b_s):
    B, S, _ = u.shape
    nc = S // CHUNK
    w = w_s * jnp.tril(jnp.ones((CHUNK, CHUNK), w_s.dtype))
    vr = vn.reshape(B, nc, CHUNK, G_A, GD_A)
    mixed = jnp.einsum('gij,bcjgd->bcigd', w, vr) + b_s.T[None, None, :, :, None]
    return u * mixed.reshape(B, S, D_A)

def gmlp_chunk_sample(u, vn, w_s, b_s):
    Bd, Sd, _ = u.shape
    w = (w_s * jnp.tril(jnp.ones((CHUNK, CHUNK), w_s.dtype)))[:, :Sd, :Sd]
    vr = vn.reshape(Bd, Sd, G_A, GD_A)
    mixed = jnp.einsum('gij,bjgd->bigd', w, vr) + b_s[:, :Sd].T[None, :, :, None]
    return u * mixed.reshape(Bd, Sd, D_A)

def dilated_branch_prompt(q, k, v, window, dil):
    B, S, H, HD = q.shape
    L = S // dil
    wn = window // dil
    nb = -(-L // QBLK)
    Lp = nb * QBLK

    def to_res(t):
        t = t.reshape(B, L, dil, H, HD).transpose(0, 2, 1, 3, 4)
        return jnp.pad(t, ((0, 0), (0, 0), (0, Lp - L), (0, 0), (0, 0)))

    def kblocks(t):
        t = jnp.pad(t, ((0, 0), (0, 0), (QBLK, 0), (0, 0), (0, 0)))
        t = t.reshape(B, dil, nb + 1, QBLK, H, HD)
        return jnp.concatenate([t[:, :, :-1], t[:, :, 1:]], axis=3)

    qb = to_res(q).reshape(B, dil, nb, QBLK, H, HD)
    kb = kblocks(to_res(k))
    vb = kblocks(to_res(v))
    s = jnp.einsum('brnqhd,brnkhd->brnhqk', qb, kb).astype(jnp.float32)
    qi = jnp.arange(QBLK)[None, :, None]
    kk = jnp.arange(2 * QBLK)[None, None, :]
    blk = jnp.arange(nb)[:, None, None]
    dist = QBLK + qi - kk
    key_idx = (blk - 1) * QBLK + kk
    valid = (dist >= 0) & (dist <= wn) & (key_idx >= 0)
    s = jnp.where(valid[None, None, :, None], s, NEG)
    m = jnp.max(s, axis=-1, keepdims=True)
    p = jnp.exp(s - m)
    den = jnp.sum(p, axis=-1)
    o = jnp.einsum('brnhqk,brnkhd->brnqhd', p.astype(v.dtype), vb)
    o = o / jnp.swapaxes(den, -1, -2)[..., None].astype(o.dtype)
    lse = m[..., 0] + jnp.log(den)
    o = o.reshape(B, dil, Lp, H, HD)[:, :, :L].transpose(0, 2, 1, 3, 4).reshape(B, S, H, HD)
    lse = jnp.swapaxes(lse, -1, -2).reshape(B, dil, Lp, H)[:, :, :L]
    lse = lse.transpose(0, 2, 1, 3).reshape(B, S, H)
    return o, lse

def dilated_branch_sample(q, k_all, v_all, window, dil, buf):
    Sd = q.shape[1]
    wn = window // dil
    idx = buf + jnp.arange(Sd)[:, None] - dil * jnp.arange(wn + 1)[None, :]
    valid = idx >= 0
    idc = jnp.clip(idx, 0, None)
    kg = k_all[:, idc]
    vg = v_all[:, idc]
    s = jnp.einsum('bqhd,bqkhd->bqhk', q, kg).astype(jnp.float32)
    s = jnp.where(valid[None, :, None, :], s, NEG)
    m = jnp.max(s, axis=-1, keepdims=True)
    p = jnp.exp(s - m)
    den = jnp.sum(p, axis=-1)
    o = jnp.einsum('bqhk,bqkhd->bqhd', p.astype(v_all.dtype), vg) / den[..., None].astype(v_all.dtype)
    lse = m[..., 0] + jnp.log(den)
    return o, lse

def combine_branches(outs, lses):
    alpha = jax.nn.softmax(jnp.stack(lses, axis=0), axis=0)
    o = jnp.sum(alpha[..., None].astype(outs[0].dtype) * jnp.stack(outs, axis=0), axis=0)
    return o.reshape(o.shape[:-2] + (D_B,))

def peer_ffn(x, w_q, sub_keys, u_tab, v_tab):
    lead = x.shape[:-1]
    xt = x.reshape(-1, D_MODEL)
    T = xt.shape[0]
    nblk = -(-T // TOK_BLK)
    xt = jnp.pad(xt, ((0, nblk * TOK_BLK - T), (0, 0))).reshape(nblk, TOK_BLK, D_MODEL)

    def block(xb):
        q = (xb @ w_q).reshape(TOK_BLK, PEER_HEADS, 2, DK_HALF)
        s = jnp.einsum('thcd,hcnd->thcn', q, sub_keys).astype(jnp.float32)
        s1, i1 = lax.top_k(s[:, :, 0], TOPK)
        s2, i2 = lax.top_k(s[:, :, 1], TOPK)
        cand = (s1[..., :, None] + s2[..., None, :]).reshape(TOK_BLK, PEER_HEADS, TOPK * TOPK)
        cid = (i1[..., :, None] * N_KEYS + i2[..., None, :]).reshape(TOK_BLK, PEER_HEADS, TOPK * TOPK)
        top_s, pos = lax.top_k(cand, TOPK)
        eid = jnp.take_along_axis(cid, pos, axis=-1)
        g = jax.nn.softmax(top_s, axis=-1).astype(xb.dtype)
        hid = jax.nn.gelu(jnp.einsum('thkd,td->thk', u_tab[eid], xb), approximate=False)
        return jnp.einsum('thk,thkd->td', g * hid, v_tab[eid])

    y = lax.map(block, xt).reshape(nblk * TOK_BLK, D_MODEL)[:T]
    return y.reshape(lead + (D_MODEL,))

def setup_inputs(seed: int = 0) -> dict:
    key = jax.random.key(seed)
    ks = jax.random.split(key, 20)
    buf = min(WIN_MAX, PAST_LEN)
    f32 = jnp.float32
    nrm = lambda k, shape, sc: jax.random.normal(k, shape, f32) * sc
    return {
        "x_prompt": nrm(ks[0], (BATCH, SEQ, D_MODEL), 1.0),
        "x_sample": nrm(ks[1], (DEC_BATCH, DEC_SEQ, D_MODEL), 1.0),
        "cache_k_win": nrm(ks[2], (DEPTH, DEC_BATCH, buf, H_B, HEAD_DIM), 1.0),
        "cache_v_win": nrm(ks[3], (DEPTH, DEC_BATCH, buf, H_B, HEAD_DIM), 1.0),
        "attn_norm": 1.0 + nrm(ks[4], (DEPTH, D_MODEL), 0.02),
        "w_in": nrm(ks[5], (DEPTH, D_MODEL, D_IN), D_MODEL ** -0.5),
        "ln_v_g": 1.0 + nrm(ks[6], (DEPTH, D_A), 0.02),
        "ln_v_b": nrm(ks[7], (DEPTH, D_A), 0.02),
        "w_s": nrm(ks[8], (DEPTH, G_A, CHUNK, CHUNK), CHUNK ** -0.5),
        "b_s": 1.0 + nrm(ks[9], (DEPTH, G_A, CHUNK), 0.1),
        "w_out": nrm(ks[10], (DEPTH, D_MIX, D_MODEL), D_MIX ** -0.5),
        "ffn_norm": 1.0 + nrm(ks[11], (DEPTH, D_MODEL), 0.02),
        "peer_w_q": nrm(ks[12], (DEPTH, D_MODEL, PEER_HEADS * D_KEY), D_MODEL ** -0.5),
        "peer_sub_keys": nrm(ks[13], (DEPTH, PEER_HEADS, 2, N_KEYS, DK_HALF), DK_HALF ** -0.5),
        "peer_u": nrm(ks[14], (DEPTH, N_EXPERTS, D_MODEL), D_MODEL ** -0.5),
        "peer_v": nrm(ks[15], (DEPTH, N_EXPERTS, D_MODEL), 0.25),
        "final_norm": 1.0 + nrm(ks[16], (D_MODEL,), 0.02),
    }

def reference(x_prompt, x_sample, cache_k_win, cache_v_win, attn_norm, w_in, ln_v_g, ln_v_b,
              w_s, b_s, w_out, ffn_norm, peer_w_q, peer_sub_keys, peer_u, peer_v, final_norm):
    S = x_prompt.shape[1]
    Sd = x_sample.shape[1]
    buf = cache_k_win.shape[2]
    buf_p = min(WIN_MAX, S)
    pos_p = jnp.arange(S)
    pos_s = PAST_LEN + jnp.arange(Sd)
    xp, xs = x_prompt, x_sample
    kp_list, vp_list, ks_list, vs_list, gv_list = [], [], [], [], []
    for l in range(DEPTH):
        h = rmsnorm(xp, attn_norm[l])
        u, vn, q, k, v = mix_projection(h, w_in[l], ln_v_g[l], ln_v_b[l], pos_p)
        a_out = gmlp_chunk_prompt(u, vn, w_s[l], b_s[l])
        res = [dilated_branch_prompt(q, k, v, w, r) for (w, r) in DILATED]
        b_out = combine_branches([o for o, _ in res], [s for _, s in res])
        xp = xp + jnp.concatenate([a_out, b_out], axis=-1) @ w_out[l]
        xp = xp + peer_ffn(rmsnorm(xp, ffn_norm[l]), peer_w_q[l], peer_sub_keys[l], peer_u[l], peer_v[l])
        kp_list.append(k[:, S - buf_p:])
        vp_list.append(v[:, S - buf_p:])
        h = rmsnorm(xs, attn_norm[l])
        u, vn, q, k, v = mix_projection(h, w_in[l], ln_v_g[l], ln_v_b[l], pos_s)
        a_out = gmlp_chunk_sample(u, vn, w_s[l], b_s[l])
        k_all = jnp.concatenate([cache_k_win[l].astype(k.dtype), k], axis=1)
        v_all = jnp.concatenate([cache_v_win[l].astype(v.dtype), v], axis=1)
        res = [dilated_branch_sample(q, k_all, v_all, w, r, buf) for (w, r) in DILATED]
        b_out = combine_branches([o for o, _ in res], [s for _, s in res])
        xs = xs + jnp.concatenate([a_out, b_out], axis=-1) @ w_out[l]
        xs = xs + peer_ffn(rmsnorm(xs, ffn_norm[l]), peer_w_q[l], peer_sub_keys[l], peer_u[l], peer_v[l])
        ks_list.append(k)
        vs_list.append(v)
        gv_list.append(vn)
    y_prompt = rmsnorm(xp, final_norm)
    y_sample = rmsnorm(xs, final_norm)
    k_win_prompt = jnp.stack(kp_list, axis=0)
    v_win_prompt = jnp.stack(vp_list, axis=0)
    k_win_sample_new = jnp.stack(ks_list, axis=0)
    v_win_sample_new = jnp.stack(vs_list, axis=0)
    gmlp_v_sample = jnp.stack(gv_list, axis=0)
    return (y_prompt, y_sample, k_win_prompt, v_win_prompt, k_win_sample_new, v_win_sample_new, gmlp_v_sample)


_drawn_inputs = setup_inputs


def setup_inputs(seed=0):
    import zlib

    import numpy as np

    out = dict(_drawn_inputs(seed))
    spreads = {}
    factors = {'attn_norm': 2.829,
     'ln_v_g': 19.484,
     'ln_v_b': 20.205,
     'ffn_norm': 9.695,
     'final_norm': 23.367}
    for name, (base, spread) in spreads.items():
        noise = np.random.default_rng([zlib.crc32(name.encode()), seed]).standard_normal(out[name].shape)
        drawn = base * np.exp(spread * noise) if base else spread * noise
        out[name] = __import__('jax').numpy.asarray(drawn.astype(out[name].dtype))
    for name, factor in factors.items():
        out[name] = (out[name] * factor).astype(out[name].dtype)
    return out
```

```python
import math
from contextlib import ExitStack

import numpy as np

import concourse.bass as bass
from concourse import mybir
from concourse.alu_op_type import AluOpType as ALU

ACT = mybir.ActivationFunctionType
AX = mybir.AxisListType
F32 = mybir.dt.float32
U32 = mybir.dt.uint32

P = 128
D = 1024
KD = D // P
SEQ = 512
NB, NS = 8, 4
NSAMP = NB * NS
PAST = 1024
DA, DB, NH, HD = 256, 768, 12, 64
GA = 4
PAIRS = NH // 2
TOK = SEQ + NSAMP
TILES = [(t * P, P) for t in range(SEQ // P)] + [(SEQ, NSAMP)]
NT = len(TILES)
SAMP = NT - 1
HALF = DB // 2
CHUNKS = [("uv", 0, 2 * DA)] + [(n, 2 * DA + i * DB + j * HALF, HALF)
                                for i, n in enumerate("qkv") for j in range(2)]
BRANCHES = ((128, 1), (512, 4), (2048, 16))
NEG = -1e30
EPS = 1e-6
STRIDED = 128
NEAR = 512
CK = STRIDED + NEAR
NEWK = NSAMP
SROWS = NH * NS
SCOLS = CK + NEWK

HEADS = 8
NKEYS = 128
TOPK = 16
SLOTS = HEADS * TOPK
UR, VR = 8, 4
GROUPS = P // NSAMP
LINKS = 13
STEPS = [HEADS] * (NT - 1) + [HEADS // GROUPS]
FIRST = [sum(STEPS[:t]) for t in range(NT)]
NSTEP = sum(STEPS)


def build(nc, x_p, x_s, k_cache, v_cache, gains, w_in, ln_gb, w_sT, b_sT, w_out, w_q, keysT, u_tab, v_tab,
          ident_c, logc_c, smask_c, snew_c, rope_c, iota_c, tril_c, blockm_c,
          y_p, y_s, k_p, v_p, k_s, v_s, gv_s):
    ctx = ExitStack()
    with ctx:
        def sb(name, n, dt=F32):
            return ctx.enter_context(nc.sbuf_tensor(name, [P, n], dt))

        def sem(name):
            return ctx.enter_context(nc.semaphore(name))

        area_w = sb("area_w", 16384)
        area_r = sb("area_r", 14720)
        area_t = sb("area_t", KD * TOK)
        area_x = sb("area_x", NT * D)
        area_v = sb("area_v", 6400)
        area_c = sb("area_c", 2176)

        def cut(area, a, *dims):
            n = math.prod(dims)
            v = area[:, a:a + n]
            if len(dims) == 2:
                v = v.rearrange("p (a b) -> p a b", a=dims[0])
            if len(dims) == 3:
                v = v.rearrange("p (a b c) -> p a b c", a=dims[0], b=dims[1])
            return v

        W_SLOTS = 4
        w_ring = [cut(area_w, s * KD * 512, KD, 512) for s in range(W_SLOTS)]
        kc = [cut(area_w, s * PAIRS * CK, PAIRS, CK) for s in range(2)]
        vc = [cut(area_w, (2 + s) * PAIRS * CK, CK // P, DB) for s in range(2)]
        wq = cut(area_w, 0, KD, 2 * HEADS * P)

        w_o = cut(area_r, 0, KD, D)
        qT = cut(area_r, KD * D, PAIRS, TOK)
        kT = cut(area_r, KD * D + PAIRS * TOK, PAIRS, TOK)
        u_ring = [cut(area_r, s * D, D) for s in range(UR)]
        v_ring = [cut(area_r, (UR + s) * D, D) for s in range(VR)]
        keys = cut(area_r, (UR + VR) * D, 2 * HEADS * NKEYS)

        featT = cut(area_t, 0, KD, TOK)

        x = cut(area_x, 0, NT, D)
        SR = 4
        q_stage = [cut(area_x, s * HALF, HALF) for s in range(3)]
        k_stage = [cut(area_x, (3 + s) * HALF, HALF) for s in range(2 * NT)]
        score = [cut(area_x, s * SCOLS, SCOLS) for s in range(SR)]
        probT = [cut(area_x, SR * SCOLS + s * 512, 512) for s in range(2)]
        QB = 344
        q_blk = [cut(area_x, SR * SCOLS + 1024 + s * QB, QB) for s in range(2)]

        def blocks_of(q, r0, c0):
            w = SROWS + 2 * NS
            v = q[r0:r0 + HD, 0:PAIRS * w + 2 * NS]
            return v[:, c0:c0 + PAIRS * w].rearrange("p (r w) -> p r w", w=w)[:, :, 0:NS]


        h_stage = [cut(area_v, s * D, D) for s in range(2)]
        v_tok = cut(area_v, 0, NT, DB)
        u_tok = cut(area_v, NT * DB, NT, DA)
        vn = cut(area_v, NT * (DB + DA), NT, DA)
        xn = cut(area_v, 0, NT, D)

        logc = cut(area_c, 0, 512)
        smask = cut(area_c, 512, CK)
        snew = cut(area_c, 512 + CK, NB, NEWK)
        lngb = cut(area_c, 512 + CK + NB * NEWK, 2, DA)

        gain = sb("gain", D)
        ident = sb("ident", P)
        w_s = sb("w_s", GA * P)
        w_s32 = sb("w_s32", GA * NS)
        w_sb = sb("w_sb", GA * NSAMP)
        bs = sb("bs", 2 * GA)
        tril = sb("tril", P)
        blockm = sb("blockm", NSAMP)
        rope = sb("rope", NT * 32)
        rope_ab = sb("rope_ab", 4 * 96)
        iota = sb("iota", TOPK)
        small = sb("small", 24)
        eps = sb("eps", 1)
        lnst = sb("lnst", NT * 8)
        att = sb("att", SR * 4)

        eid = sb("eid", NSTEP * TOPK, U32)
        gate = sb("gate", NSTEP * TOPK)
        u_idx = sb("u_idx", UR, U32)
        v_idx = sb("v_idx", VR, U32)
        hid = sb("hid", TOPK)
        gelu = sb("gelu", TOPK)
        wts = sb("wts", TOPK)
        ident4 = sb("ident4", NSAMP)

        diag = [cut(area_c, s * P, P) for s in range(VR)]
        q_row = cut(area_c, 512, 2 * P)
        q_col = cut(area_c, 768, 2, P)
        s_cur = cut(area_v, NT * D, 2, NKEYS)
        s_left = cut(area_v, NT * D + 256, 2, NKEYS)
        cand = cut(area_c, 1024, TOPK * TOPK)
        cand_left = cut(area_c, 1280, TOPK * TOPK)
        hot = [cut(area_v, NT * D + 512 + c * 256, TOPK, TOPK) for c in range(2)]
        tops = cut(area_c, 1536, HEADS, TOPK)
        eid_samp = cut(area_c, 1664, SLOTS)
        gate_samp = cut(area_c, 1792, SLOTS)
        rt = cut(area_c, 1920, 9 * TOPK)
        rtu = sb("rtu", 5 * TOPK, U32)
        val = [rt[:, c * TOPK:(c + 1) * TOPK] for c in range(2)]
        idf = [rt[:, (2 + c) * TOPK:(3 + c) * TOPK] for c in range(2)]
        pick = [rt[:, (4 + c) * TOPK:(5 + c) * TOPK] for c in range(2)]
        top = rt[:, 6 * TOPK:7 * TOPK]
        den8 = rt[:, 7 * TOPK:7 * TOPK + 8]
        rden8 = rt[:, 7 * TOPK + 8:8 * TOPK]
        eidf = rt[:, 8 * TOPK:9 * TOPK]
        idx = [rtu[:, c * TOPK:(c + 1) * TOPK] for c in range(2)]
        pos = rtu[:, 2 * TOPK:3 * TOPK]
        digit = [rtu[:, (3 + c) * TOPK:(4 + c) * TOPK] for c in range(2)]

        bank = [ctx.enter_context(nc.psum_tensor(f"bank{i}", [P, 2, 512], F32)) for i in range(4)]

        def half(i):
            return bank[i // 2][:, i % 2, :]

        def wide(i, n):
            return bank[i].rearrange("p a b -> p (a b)")[:, 0:n]

        acc = bank[0]
        x_cur = wide(1, D)
        ps_q, ps_qT, ps_s = half(4), half(5), half(6)

        x_in = [sem(f"x_in{t}") for t in range(NT)]
        x_again = sem("x_again")
        consts_in, gain_in = sem("consts_in"), sem("gain_in")
        w_in_sem = [sem(f"w_in{s}") for s in range(W_SLOTS)]
        w_out_in, wq_in, keys_in = sem("w_out_in"), sem("wq_in"), sem("keys_in")
        kc_in = [sem(f"kc_in{s}") for s in range(2)]
        vc_in = [sem(f"vc_in{s}") for s in range(2)]
        kv_out, y_out = sem("kv_out"), sem("y_out")
        dv = sem("dv")
        eps_set, summed, ln_stats, ln_root = sem("eps_set"), sem("summed"), sem("ln_stats"), sem("ln_root")
        squared, h_ready, h_turned, hT_ready = sem("squared"), sem("h_ready"), sem("h_turned"), sem("hT_ready")
        proj_done, uv_read, qkv_read = sem("proj_done"), sem("uv_read"), sem("qkv_read")
        roped, qk_turned, qkT_ready = sem("roped"), sem("qk_turned"), sem("qkT_ready")
        ws_ready, mixed_done, gated, g_turned, gT_ready = (sem("ws_ready"), sem("mixed_done"), sem("gated"),
                                                           sem("g_turned"), sem("gT_ready"))
        qb_ready, scored, masked, exped, normed = (sem("qb_ready"), sem("scored"), sem("masked"), sem("exped"),
                                                   sem("normed"))
        p_turned, pT_ready, pv_done, att_ready = sem("p_turned"), sem("pT_ready"), sem("pv_done"), sem("att_ready")
        out_done, x2_ready, squared2, xn_ready = sem("out_done"), sem("x2_ready"), sem("squared2"), sem("xn_ready")
        xn_turned, xnT_ready = sem("xn_turned"), sem("xnT_ready")
        qz = sem("qz")
        q_done, q_copied, q_turned, qT_copied = sem("q_done"), sem("q_copied"), sem("q_turned"), sem("qT_copied")
        s_done, s_ready = sem("s_done"), sem("s_ready")
        tops_exped = sem("tops_exped")
        u_landed = [sem(f"u_landed{s}") for s in range(UR)]
        v_landed = [sem(f"v_landed{s}") for s in range(VR)]
        u_free, v_free = sem("u_free"), sem("v_free")
        staged = sem("staged")
        gelu_done, w_ready, diag_ready = sem("gelu_done"), sem("w_ready"), sem("diag_ready")
        passed = sem("passed")
        eid_ready, eid_samp_ready = sem("eid_ready"), sem("eid_samp_ready")
        route_link = sem("route_link")
        acc_read, y_squared, y_ready = sem("acc_read"), sem("y_squared"), sem("y_ready")

        block = ctx.enter_context(nc.Block())

        N_CONST = 1 + 1 + NT + 1 + 2 * NB + 7 + GROUPS
        UNITS = [(c, t) for c in range(len(CHUNKS)) for t in range(NT)]
        QK = [(c, t) for c, t in UNITS if CHUNKS[c][0] in "qk"]
        qk_at = {u: i for i, u in enumerate(QK)}
        N_QKV = len(UNITS) - NT
        ATT = []
        for i in range(NH * (NT - 1)):
            ATT.append((i // (NT - 1), i % (NT - 1)))
            if i % 6 == 5:
                ATT.append(("s", i // 6))
        samp_at = {b: ATT.index(("s", b)) for b in range(NB)}
        NOUT = 2 * 2 * NT
        MIXED = NT

        def span(u):
            return (P, (u[1] + 1) * P) if u[0] != "s" else (SROWS, SCOLS)

        def wait_apart(engine, what, value):
            engine.wait_ge(what, value)
            engine.sem_inc(passed, 1)

        def peer_x(t):
            return NSAMP if t == SAMP else P

        @block.sync
        def _(sp):
            for t, (a, n) in enumerate(TILES):
                src = x_p[a:a + n, :] if t < SAMP else x_s
                sp.dma_start(x[0:n, t, :], src).then_inc(x_in[t], 16)
                if t == 0:
                    sp.dma_start(gain[:], gains[0:1, :].broadcast_to([P, D])).then_inc(gain_in, 16)
                    sp.dma_start(ident[:], ident_c).then_inc(consts_in, 16)

            def load_w(c):
                s = c % W_SLOTS
                _, a, n = CHUNKS[c]
                sp.dma_start(w_ring[s][:, :, 0:n],
                             w_in[:, a:a + n].rearrange("(k p) n -> p k n", p=P)).then_inc(w_in_sem[s], 16)

            load_w(0)
            sp.dma_start(lngb, ln_gb.rearrange("(o a) d -> o a d", o=1).broadcast_to([P, 2, DA])).then_inc(consts_in, 16)
            for t, (a, n) in enumerate(TILES):
                sp.dma_start(rope[0:n, 32 * t:32 * t + 32], rope_c[a:a + n, :]).then_inc(consts_in, 16)
            load_w(1)
            sp.dma_start(w_s[:].rearrange("p (g i) -> p g i", g=GA), w_sT.rearrange("g j i -> j g i")).then_inc(consts_in, 16)
            for b in range(NB):
                sp.dma_start(w_s32[b * NS:(b + 1) * NS, :].rearrange("p (g i) -> p g i", g=GA),
                             w_sT[:, 0:NS, 0:NS].rearrange("g j i -> j g i")).then_inc(consts_in, 16)
                sp.dma_start(bs[b * NS:(b + 1) * NS, GA:2 * GA], b_sT[0:NS, :]).then_inc(consts_in, 16)
            sp.dma_start(bs[:, 0:GA], b_sT).then_inc(consts_in, 16)
            sp.dma_start(tril[:], tril_c).then_inc(consts_in, 16)
            sp.dma_start(blockm[0:NSAMP, :], blockm_c).then_inc(consts_in, 16)
            sp.dma_start(iota[:], iota_c).then_inc(consts_in, 16)
            sp.dma_start(logc, logc_c).then_inc(consts_in, 16)
            sp.dma_start(smask[0:SROWS, :], smask_c).then_inc(consts_in, 16)
            sp.dma_start(snew[0:SROWS], snew_c).then_inc(consts_in, 16)
            for g in range(GROUPS):
                sp.dma_start(ident4[g * NSAMP:(g + 1) * NSAMP, :], ident_c[0:NSAMP, 0:NSAMP]).then_inc(consts_in, 16)
            load_w(2)
            load_w(3)
            sp.dma_start(w_o, w_out.rearrange("(k p) n -> p k n", p=P)).then_inc(w_out_in, 16)
            for c in range(W_SLOTS, len(CHUNKS)):
                sp.wait_ge(proj_done, NT * (c - W_SLOTS + 1))
                load_w(c)
            sp.wait_ge(h_ready, NT)
            sp.dma_start(gain[:], gains[1:2, :].broadcast_to([P, D])).then_inc(gain_in, 16)
            for c, t in QK:
                if CHUNKS[c][0] == "k":
                    i, (a, n) = qk_at[c, t], TILES[t]
                    sp.wait_ge(roped, i + 1)
                    dst, a = (k_p, a) if t < SAMP else (k_s, 0)
                    j = CHUNKS[c][1] - 2 * DA - DB
                    sp.dma_start(dst[a:a + n, j:j + HALF], k_stage[i - 2 * NT][0:n, :]).then_inc(kv_out, 16)
            sp.wait_ge(qkv_read, N_QKV)
            for t, (a, n) in enumerate(TILES):
                dst, a = (v_p, a) if t < SAMP else (v_s, 0)
                sp.dma_start(dst[a:a + n, :], v_tok[0:n, t, :]).then_inc(kv_out, 16)
            sp.dma_start(gv_s, vn[0:NSAMP, SAMP, :]).then_inc(kv_out, 16)
            sp.wait_ge(proj_done, len(UNITS))
            for b in range(NB):
                s = b % 2
                if b >= 2:
                    sp.wait_ge(scored, samp_at[b - 2] + 1)
                sp.dma_start(kc[s], k_cache[b][:, 0:CK].rearrange("(r p) n -> p r n", p=P)).then_inc(kc_in[s], 16)
                if b >= 2:
                    sp.wait_ge(pv_done, samp_at[b - 2] + 1)
                sp.dma_start(vc[s], v_cache[b][0:CK, :].rearrange("(c p) n -> p c n", p=P)).then_inc(vc_in[s], 16)
            sp.wait_ge(pv_done, len(ATT))
            sp.wait_ge(qb_ready, NB)
            for t, (a, n) in enumerate(TILES):
                src = x_p[a:a + n, :] if t < SAMP else x_s
                sp.dma_start(x[0:n, t, :], src).then_inc(x_again, 16)
            sp.dma_start(wq, w_q.rearrange("(k p) n -> p k n", p=P)).then_inc(wq_in, 16)
            sp.dma_start(keys, keysT).then_inc(keys_in, 16)
            sp.wait_ge(xn_ready, NT)
            sp.dma_start(gain[:], gains[2:3, :].broadcast_to([P, D])).then_inc(gain_in, 16)
            for t, (a, n) in enumerate(TILES):
                sp.wait_ge(y_ready, t + 1)
                dst = y_p[a:a + n, :] if t < SAMP else y_s
                sp.dma_start(dst, x[0:n, t, :]).then_inc(y_out, 16)
            sp.wait_ge(y_out, 16 * NT)
            sp.wait_ge(kv_out, 16 * (2 * NT + NT + 1))

        @block.tensor
        def _(pe):
            pe.wait_ge(consts_in, 16 * N_CONST)

            def turn(out, src, n):
                return pe.transpose(out, src, ident[0:n, 0:n])

            for t, (a, n) in enumerate(TILES):
                pe.wait_ge(h_ready, t + 1)
                if t >= 2:
                    pe.wait_ge(hT_ready, t - 1)
                dst = bank[2 + t % 2]
                for k in range(KD):
                    mm = turn(dst[:, k // 4, (k % 4) * P:(k % 4) * P + n], h_stage[t % 2][0:n, k * P:(k + 1) * P], n)
                mm.then_inc(h_turned, 1)

            def turn_qk(i):
                c, t = QK[i]
                n = TILES[t][1]
                pe.wait_ge(roped, i + 1)
                if i >= 2:
                    pe.wait_ge(qkT_ready, i - 1)
                else:
                    pe.wait_ge(hT_ready, NT)
                src = q_stage[i % 3] if CHUNKS[c][0] == "q" else k_stage[i - 2 * NT]
                for j in range(3):
                    mm = turn(half(4 + i % 2)[:, j * P:j * P + n], src[0:n, j * P:(j + 1) * P], n)
                mm.then_inc(qk_turned, 1)

            for u, (c, t) in enumerate(UNITS):
                a, n = TILES[t]
                w = CHUNKS[c][2]
                if t == 0:
                    pe.wait_ge(w_in_sem[c % W_SLOTS], 16 * (c // W_SLOTS + 1))
                if c == 0:
                    pe.wait_ge(hT_ready, t + 1)
                if 3 <= u < NT + 3:
                    pe.wait_ge(uv_read, u - 2)
                elif u >= NT + 3:
                    pe.wait_ge(qkv_read, u - 2 - NT)
                for k in range(KD):
                    mm = pe.matmul(half(u % 3)[0:n, 0:w], featT[:, k, a:a + n], w_ring[c % W_SLOTS][:, k, 0:w],
                                   start=(k == 0), stop=(k == KD - 1))
                mm.then_inc(proj_done, 1)
                if u >= 2 and UNITS[u - 2] in qk_at:
                    turn_qk(qk_at[UNITS[u - 2]])

            pe.wait_ge(ws_ready, 1)
            pe.wait_ge(qkT_ready, len(QK))

            def gmlp(t):
                n = TILES[t][1]
                if t >= 2:
                    pe.wait_ge(gated, t - 1)
                for g in range(GA):
                    lhs = w_s[:, g * P:(g + 1) * P] if t < SAMP else w_sb[0:n, g * NSAMP:(g + 1) * NSAMP]
                    mm = pe.matmul(half(4 + t % 2)[0:n, g * HD:(g + 1) * HD], lhs, vn[0:n, t, g * HD:(g + 1) * HD],
                                   start=True, stop=True)
                mm.then_inc(mixed_done, 1)

            def turn_gated(t):
                n = TILES[t][1]
                pe.wait_ge(gated, t + 1)
                if t >= 2:
                    pe.wait_ge(gT_ready, t - 1)
                for k in range(2):
                    mm = turn(half(6 + t % 2)[:, k * P:k * P + n], u_tok[0:n, t, k * P:(k + 1) * P], n)
                mm.then_inc(g_turned, 1)

            for t in range(MIXED + 1):
                if t < MIXED:
                    gmlp(t)
                if t >= 1:
                    turn_gated(t - 1)
            pe.wait_ge(gT_ready, NT)
            pe.wait_ge(qkv_read, N_QKV)

            def scores(u):
                unit = ATT[u]
                if u >= 2:
                    pe.wait_ge(masked, u - 1)
                if unit[0] != "s":
                    h, t = unit
                    r0, pr = HD * (h % 2), h // 2
                    n = (t + 1) * P
                    mm = pe.matmul(wide(u % 2, n), qT[r0:r0 + HD, pr, t * P:(t + 1) * P], kT[r0:r0 + HD, pr, 0:n],
                                   start=True, stop=True)
                else:
                    b = unit[1]
                    pe.wait_ge(qb_ready, b + 1)
                    pe.wait_ge(kc_in[b % 2], 16 * (b // 2 + 1))
                    for lo, hi, src in ((0, 512, kc[b % 2][:, :, 0:512]), (512, CK, kc[b % 2][:, :, 512:CK]),
                                        (CK, SCOLS, kT[:, :, SEQ:TOK])):
                        for pr in range(PAIRS):
                            mm = pe.matmul(wide(u % 2, D)[0:SROWS, lo:hi], q_blk[b % 2][:, pr * SROWS:(pr + 1) * SROWS],
                                           src[:, pr, :], start=(pr == 0), stop=(pr == PAIRS - 1))
                mm.then_inc(scored, 1)

            def turn_probs(u):
                r, n = span(ATT[u])
                pe.wait_ge(normed, u + 1)
                if u >= 2:
                    pe.wait_ge(pT_ready, u - 1)
                for j, a in enumerate(range(0, n, P)):
                    w = min(P, n - a)
                    mm = turn(half(4 + u % 2)[0:w, j * r:(j + 1) * r], score[u % SR][0:r, a:a + w], r)
                mm.then_inc(p_turned, 1)

            def outputs(u):
                unit = ATT[u]
                out = half(6 + u % 2)
                pe.wait_ge(pT_ready, u + 1)
                if u >= 2:
                    pe.wait_ge(att_ready, u - 1)
                if unit[0] != "s":
                    h, t = unit
                    r0 = HD * (h % 2)
                    for j in range(t + 1):
                        mm = pe.matmul(out[r0:r0 + HD, 0:P], v_tok[:, j, h * HD:(h + 1) * HD],
                                       probT[u % 2][:, j * P:(j + 1) * P], start=(j == 0), stop=(j == t))
                else:
                    b = unit[1]
                    pe.wait_ge(vc_in[b % 2], 16 * (b // 2 + 1))
                    for pr in range(PAIRS):
                        for j in range(CK // P + 1):
                            new = j == CK // P
                            lhs = (v_tok[0:NEWK, SAMP, pr * P:(pr + 1) * P] if new
                                   else vc[b % 2][:, j, pr * P:(pr + 1) * P])
                            rhs = probT[u % 2][0:NEWK if new else P, j * SROWS + pr * 8:j * SROWS + pr * 8 + 8]
                            mm = pe.matmul(out[:, pr * 8:pr * 8 + 8], lhs, rhs, start=(j == 0), stop=new)
                mm.then_inc(pv_done, 1)

            for u in range(len(ATT) + 3):
                if u < len(ATT):
                    scores(u)
                if 2 <= u < len(ATT) + 2:
                    turn_probs(u - 2)
                if u >= 3:
                    outputs(u - 3)

            def turn_xn(t):
                a, n = TILES[t]
                pe.wait_ge(xn_ready, t + 1)
                if t >= 2:
                    pe.wait_ge(xnT_ready, t - 1)
                for k in range(KD):
                    mm = turn(bank[2 + t % 2][:, k // 4, (k % 4) * P:(k % 4) * P + n], xn[0:n, t, k * P:(k + 1) * P], n)
                mm.then_inc(xn_turned, 1)

            pe.wait_ge(w_out_in, 16)
            pe.wait_ge(att_ready, len(ATT))
            pe.wait_ge(masked, len(ATT))
            for t in range(NT + 1):
                if t < NT:
                    a, n = TILES[t]
                    if t >= 2:
                        pe.wait_ge(x2_ready, t - 1)
                    for c in range(2):
                        for k in range(KD):
                            mm = pe.matmul(bank[t % 2][0:n, c, :], featT[:, k, a:a + n], w_o[:, k, c * 512:(c + 1) * 512],
                                           start=(k == 0), stop=(k == KD - 1))
                    mm.then_inc(out_done, 1)
                if t >= 1:
                    turn_xn(t - 1)

            def queries(t, h, n_done):
                a, n = TILES[t]
                if not isinstance(n_done, int) or n_done:
                    pe.wait_ge(q_copied, n_done)
                for k in range(KD):
                    mm = pe.matmul(ps_q[0:n, 0:2 * P], featT[:, k, a:a + n], wq[:, k, bass.ds(h * 2 * P, 2 * P)],
                                   start=(k == 0), stop=(k == KD - 1))
                mm.then_inc(q_done, 1)

            def turn_queries(t, n_done):
                n = TILES[t][1]
                wait_apart(pe, q_copied, n_done + 1)
                for c in range(2):
                    mm = turn(ps_qT[:, c * P:c * P + n], q_row[0:n, c * P:(c + 1) * P], n)
                mm.then_inc(q_turned, 1)

            def key_scores(t, h, n_done):
                n = TILES[t][1]
                pe.wait_ge(qT_copied, n_done + 1)
                if not isinstance(n_done, int) or n_done:
                    pe.wait_ge(s_ready, n_done)
                for c in range(2):
                    mm = pe.matmul(ps_s[0:n, c * NKEYS:(c + 1) * NKEYS], q_col[:, c, 0:n],
                                   keys[:, bass.ds((2 * h + c) * NKEYS, NKEYS)], start=True, stop=True)
                mm.then_inc(s_done, 1)

            def slot(t, g, j):
                n = peer_x(t)
                s = j % VR
                pe.wait_ge(diag_ready, g * TOPK + j + 1)
                pe.wait_ge(v_landed[s], (g * (TOPK // VR) + j // VR + 1) * 16)
                for c in range(2):
                    mm = pe.matmul(acc[0:n, c, :], diag[s][:, 0:n], v_ring[s][:, c * 512:(c + 1) * 512],
                                   start=False, stop=False, skip_group_check=True)
                mm.then_inc(v_free, 1)

            def step(t, g, nxt):
                for j in range(TOPK):
                    slot(t, g, j)
                    if nxt and j == 3:
                        queries(nxt[0], nxt[1], nxt[2])
                    if nxt and j == 7:
                        turn_queries(nxt[0], nxt[2])
                    if nxt and j == 11:
                        key_scores(nxt[0], nxt[1], nxt[2])

            pe.wait_ge(xnT_ready, NT)
            pe.wait_ge(wq_in, 16)
            pe.wait_ge(keys_in, 16)
            for h in range(HEADS + 1):
                queries(h // HEADS, h % HEADS, h)
                turn_queries(h // HEADS, h)
                key_scores(h // HEADS, h % HEADS, h)
            for t in range(NT):
                a, n = TILES[t]
                if t >= 1:
                    pe.wait_ge(acc_read, t)
                else:
                    pe.wait_ge(x2_ready, NT)
                for c in range(2):
                    mm = pe.matmul(acc[0:n, c, :], ident[0:n, 0:n], x[0:n, t, c * 512:(c + 1) * 512],
                                   start=True, stop=False, skip_group_check=True)
                if t == 0:
                    mm.then_inc(v_free, VR)
                last = STEPS[t] - 1
                with pe.Fori(0, last) as i:
                    step(t, i + FIRST[t], (t + 1, i + 1, i + FIRST[t] + HEADS + 1) if t < SAMP else None)
                step(t, last + FIRST[t], (t + 2, 0, last + FIRST[t] + HEADS + 1) if t + 2 < NT else None)

        @block.scalar
        def _(act):
            def copy(out, src, scale=1.0):
                return nc.scalar.activation(out, src, ACT.Copy, scale=scale)

            ssq, rms = small[:, 0:8], small[:, 8:16]

            def root(t, summed, k, done):
                n = TILES[t][1]
                act.wait_ge(summed, k + 1)
                nc.scalar.activation(rms[0:n, t:t + 1], ssq[0:n, t:t + 1], ACT.Sqrt, scale=1.0 / D,
                                     bias=eps[0:n, :]).then_inc(done, 1)

            def square(t):
                n = TILES[t][1]
                act.wait_ge(x_in[t], 16)
                if t >= 2:
                    act.wait_ge(h_turned, t - 1)
                nc.scalar.activation(h_stage[t % 2][0:n, :], x[0:n, t, :], ACT.Square,
                                     accum_out=ssq[0:n, t:t + 1]).then_inc(summed, 1)
                root(t, summed, t, squared)

            def copy_turned(t, src_done, done):
                a, n = TILES[t]
                act.wait_ge(src_done, t + 1)
                for c in range(2):
                    src = bank[2 + t % 2][:, c, :].rearrange("p (k n) -> p k n", k=4)[:, :, 0:n]
                    ins = copy(featT[:, 4 * c:4 * c + 4, a:a + n], src)
                ins.then_inc(done, 1)

            act.wait_ge(eps_set, 1)
            for t in range(NT + 1):
                if t < NT:
                    square(t)
                if t >= 1:
                    copy_turned(t - 1, h_turned, hT_ready)

            def copy_qkT(i):
                c, t = QK[i]
                a, n = TILES[t]
                act.wait_ge(qk_turned, i + 1)
                dst = qT if CHUNKS[c][0] == "q" else kT
                b = (c - 1) % 2 * 3
                src = half(4 + i % 2)[:, 0:3 * P].rearrange("p (k n) -> p k n", k=3)[:, :, 0:n]
                copy(dst[:, b:b + 3, a:a + n], src).then_inc(qkT_ready, 1)

            for u, (c, t) in enumerate(UNITS):
                kind = CHUNKS[c][0]
                n = TILES[t][1]
                if kind == "uv":
                    st = lnst[0:n, 8 * t:8 * t + 8]
                    act.wait_ge(ln_stats, t + 1)
                    nc.scalar.activation(st[:, 5:6], st[:, 7:8], ACT.Sqrt, bias=eps[0:n, :]).then_inc(ln_root, 1)
                else:
                    act.wait_ge(proj_done, u + 1)
                    if kind == "v":
                        dst = v_tok[0:n, t, (c - 5) * HALF:(c - 4) * HALF]
                    else:
                        i = qk_at[c, t]
                        if kind == "q" and i >= 3:
                            act.wait_ge(qk_turned, i - 2)
                        dst = (q_stage[i % 3] if kind == "q" else k_stage[i - 2 * NT])[0:n, :]
                    copy(dst, half(u % 3)[0:n, 0:HALF], HD ** -0.5 if kind == "q" else 1.0).then_inc(qkv_read, 1)
                if u >= 2 and UNITS[u - 2] in qk_at:
                    copy_qkT(qk_at[UNITS[u - 2]])

            for t, (a, n) in enumerate(TILES):
                act.wait_ge(g_turned, t + 1)
                src = half(6 + t % 2)[:, 0:2 * P].rearrange("p (k n) -> p k n", k=2)[:, :, 0:n]
                copy(featT[:, 0:2, a:a + n], src).then_inc(gT_ready, 1)

            def exps(u):
                r, n = span(ATT[u])
                act.wait_ge(masked, u + 1)
                st = att[:, 4 * (u % SR):4 * (u % SR) + 4]
                nc.scalar.activation(score[u % SR][0:r, 0:n], score[u % SR][0:r, 0:n], ACT.Exp, bias=st[0:r, 0:1],
                                     scale=-1.0, accum_out=st[0:r, 2:3]).then_inc(exped, 1)

            def copy_pT(u):
                r, n = span(ATT[u])
                act.wait_ge(p_turned, u + 1)
                if u >= 2:
                    act.wait_ge(pv_done, u - 1)
                if ATT[u][0] != "s":
                    copy(probT[u % 2][:, 0:n], half(4 + u % 2)[:, 0:n]).then_inc(pT_ready, 1)
                else:
                    m = CK // P * SROWS
                    copy(probT[u % 2][:, 0:m], half(4 + u % 2)[:, 0:m])
                    copy(probT[u % 2][0:NEWK, m:m + SROWS], half(4 + u % 2)[0:NEWK, m:m + SROWS]).then_inc(pT_ready, 1)

            for u in range(len(ATT) + 2):
                if u < len(ATT):
                    exps(u)
                if u >= 2:
                    copy_pT(u - 2)

            act.wait_ge(pv_done, len(ATT))
            act.wait_ge(kv_out, 16 * (3 * NT + 1))
            for t in range(NT + 1):
                if t < NT:
                    n = TILES[t][1]
                    act.wait_ge(x2_ready, t + 1)
                    nc.scalar.activation(xn[0:n, t, :], x[0:n, t, :], ACT.Square,
                                         accum_out=ssq[0:n, t:t + 1]).then_inc(summed, 1)
                    root(t, summed, NT + t, squared2)
                if t >= 1:
                    copy_turned(t - 1, xn_turned, xnT_ready)

            def copy_q(t, k):
                n = TILES[t][1]
                act.wait_ge(q_done, k + 1)
                copy(q_row[0:n, :], ps_q[0:n, 0:2 * P]).then_inc(q_copied, 1)

            def copy_qT(t, k):
                n = TILES[t][1]
                act.wait_ge(q_turned, k + 1)
                copy(q_col[:, :, 0:n], ps_qT[:, 0:2 * P].rearrange("p (c n) -> p c n", c=2)[:, :, 0:n]).then_inc(qT_copied, 1)

            def copy_s(t, k):
                n = TILES[t][1]
                act.wait_ge(s_done, k + 1)
                if not isinstance(k, int) or k:
                    act.wait_ge(route_link, k * LINKS)
                copy(s_cur[0:n], ps_s[0:n, 0:2 * NKEYS].rearrange("p (c n) -> p c n", c=2)).then_inc(s_ready, 1)

            def exp_tops(t):
                n = TILES[t][1]
                act.wait_ge(route_link, (t + 1) * HEADS * LINKS)
                nc.scalar.activation(tops[0:n], tops[0:n], ACT.Exp).then_inc(tops_exped, 1)

            def step(t, g, nxt, gates_of):
                n = peer_x(t)
                act.wait_ge(u_free, UR + (g + 1) * TOPK)
                nc.scalar.activation(gelu[:], hid[:], ACT.Gelu).then_inc(gelu_done, 1)
                act.wait_ge(w_ready, g + 1)
                for j in range(TOPK):
                    act.wait_ge(v_free, g * TOPK + j + 1)
                    eye = ident if t < SAMP else ident4
                    nc.scalar.activation(diag[j % VR][:, 0:n], eye[:, 0:n], ACT.Copy,
                                         scale=wts[:, j:j + 1]).then_inc(diag_ready, 1)
                    if gates_of is not None and j == 2:
                        exp_tops(gates_of)
                    if nxt and j == 7:
                        copy_q(nxt[0], nxt[1])
                    if nxt and j == 11:
                        copy_qT(nxt[0], nxt[1])
                if nxt:
                    copy_s(nxt[0], nxt[1])

            act.wait_ge(gated, NT)
            for k in range(HEADS + 1):
                copy_q(k // HEADS, k)
                copy_qT(k // HEADS, k)
                copy_s(k // HEADS, k)
                if k == HEADS - 1:
                    exp_tops(0)
            for t in range(NT):
                n = TILES[t][1]
                last = STEPS[t] - 1
                with act.Fori(0, last) as i:
                    step(t, i + FIRST[t], (t + 1, i + FIRST[t] + HEADS + 1) if t < SAMP else None, None)
                step(t, last + FIRST[t], (t + 2, last + FIRST[t] + HEADS + 1) if t + 2 < NT else None,
                     t + 1 if t < SAMP else None)
                act.wait_ge(v_free, VR + (FIRST[t] + STEPS[t]) * TOPK)
                copy(x[0:n, t, :], acc[0:n].rearrange("p a b -> p (a b)")).then_inc(acc_read, 1)
                act.wait_ge(acc_read, t + 1)
                nc.scalar.activation(xn[0:n, t, :], x[0:n, t, :], ACT.Square,
                                     accum_out=ssq[0:n, t:t + 1]).then_inc(summed, 1)
                root(t, summed, 2 * NT + t, y_squared)

        @block.vector
        def _(dve):
            made_ops = [0]
            vec = nc.vector

            def then(ins):
                made_ops[0] += 1
                ins.then_inc(dv, 1)
                dve.wait_ge(dv, made_ops[0])

            rms, rstd = small[:, 8:16], small[:, 16:24]

            def scaled_norm(t, out, src):
                n = TILES[t][1]
                then(vec.reciprocal(rstd[0:n, t:t + 1], rms[0:n, t:t + 1]))
                return vec.scalar_tensor_tensor(out=out, in0=src, scalar=rstd[0:n, t:t + 1], in1=gain[0:n, :],
                                                op0=ALU.mult, op1=ALU.mult)

            vec.memset(eps[:], EPS).then_inc(eps_set, 1)
            dve.wait_ge(gain_in, 16)
            for t, (a, n) in enumerate(TILES):
                dve.wait_ge(squared, t + 1)
                scaled_norm(t, h_stage[t % 2][0:n, :], x[0:n, t, :]).then_inc(h_ready, 1)

            dve.wait_ge(consts_in, 16 * N_CONST)
            w3 = w_s[:].rearrange("p (g i) -> p g i", g=GA)
            vec.tensor_tensor(w3, w3, tril[:].unsqueeze(1).to_broadcast([P, GA, P]), ALU.mult)
            vec.tensor_tensor(
                w_sb[0:NSAMP, :].rearrange("p (g b i) -> p g b i", g=GA, b=NB),
                blockm[0:NSAMP, :].rearrange("p (o b i) -> p o b i", o=1, b=NB).to_broadcast([NSAMP, GA, NB, NS]),
                w_s32[0:NSAMP, :].rearrange("p (g o i) -> p g o i", g=GA, o=1).to_broadcast([NSAMP, GA, NB, NS]),
                ALU.mult).then_inc(ws_ready, 1)

            def split_uv(t, u):
                n = TILES[t][1]
                ps = half(u % 3)
                st = lnst[0:n, 8 * t:8 * t + 8]
                dve.wait_ge(proj_done, u + 1)
                vec.tensor_copy(u_tok[0:n, t, :], ps[0:n, 0:DA])
                then(vec.bn_stats(st[:, 0:6], ps[0:n, DA:2 * DA]))
                vec.bn_aggr(st[:, 6:8], st[:, 0:6]).then_inc(ln_stats, 1)
                dve.wait_ge(ln_root, t + 1)
                then(vec.reciprocal(st[:, 7:8], st[:, 5:6]))
                v = vn[0:n, t, :]
                ins = vec.tensor_scalar(v, ps[0:n, DA:2 * DA], st[:, 6:7], st[:, 7:8], ALU.subtract, ALU.mult)
                ins.then_inc(uv_read, 1)
                dve.wait_ge(uv_read, t + 1)
                then(vec.tensor_tensor(v, v, lngb[0:n, 0, :], ALU.mult))
                then(vec.tensor_tensor(v, v, lngb[0:n, 1, :], ALU.add))

            def rotate(i, u):
                c, t = QK[i]
                n = TILES[t][1]
                nh = HALF // HD
                dve.wait_ge(qkv_read, u + 1 - NT)
                src = q_stage[i % 3] if CHUNKS[c][0] == "q" else k_stage[i - 2 * NT]
                xr = src[0:n, :].rearrange("p (h d) -> p h d", d=HD)
                ab = rope_ab[0:n, (i % 2) * 192:(i % 2) * 192 + 192].rearrange("p (a h d) -> p a h d", a=2, h=nh)
                cs = rope[0:n, 32 * t:32 * t + 32].rearrange("p (a o d) -> p a o d", a=4, o=1)
                vec.tensor_tensor(ab[:, 0], xr[:, :, 0:16],
                                  rope[0:n, 32 * t:32 * t + 16].unsqueeze(1).to_broadcast([n, nh, 16]), ALU.mult)
                vec.tensor_tensor(ab[:, 1, :, 0:8], xr[:, :, 8:16], cs[:, 2].to_broadcast([n, nh, 8]), ALU.mult)
                then(vec.tensor_tensor(ab[:, 1, :, 8:16], xr[:, :, 0:8], cs[:, 3].to_broadcast([n, nh, 8]), ALU.mult))
                vec.tensor_tensor(xr[:, :, 0:16], ab[:, 0], ab[:, 1], ALU.add).then_inc(roped, 1)

            for u, (c, t) in enumerate(UNITS):
                if CHUNKS[c][0] == "uv":
                    split_uv(t, u)
                elif (c, t) in qk_at:
                    rotate(qk_at[c, t], u)

            for t, (a, n) in enumerate(TILES):
                dve.wait_ge(mixed_done, t + 1)
                b0 = 0 if t < SAMP else GA
                ps = half(4 + t % 2)[0:n, 0:DA].rearrange("p (g d) -> p g d", g=GA)
                then(vec.tensor_tensor(ps, ps, bs[0:n, b0:b0 + GA].unsqueeze(2).to_broadcast([n, GA, HD]), ALU.add))
                u3 = u_tok[0:n, t, :]
                vec.tensor_tensor(u3, u3, half(4 + t % 2)[0:n, 0:DA], ALU.mult).then_inc(gated, 1)

            dve.wait_ge(kv_out, 16 * (3 * NT + 1))
            dve.wait_ge(qkT_ready, len(QK))

            def mask_max(u):
                unit = ATT[u]
                r, n = span(unit)
                st = att[:, 4 * (u % SR):4 * (u % SR) + 4]
                dve.wait_ge(scored, u + 1)
                if u >= SR:
                    dve.wait_ge(p_turned, u - SR + 1)

                def negated(out, scores, counts, least):
                    return vec.tensor_tensor_reduce(out=out, in0=scores, in1=counts, scale=-1.0, scalar=3e38,
                                                    op0=ALU.add, op1=ALU.min, accum_out=least)

                if unit[0] != "s":
                    negated(score[u % SR][:, 0:n], wide(u % 2, n), logc[:, 512 - n:512], st[:, 0:1]).then_inc(masked, 1)
                else:
                    b = unit[1]
                    negated(score[u % SR][0:r, 0:CK], wide(u % 2, CK)[0:r], smask[0:r, :], st[0:r, 1:2])
                    then(negated(score[u % SR][0:r, CK:n], wide(u % 2, n)[0:r, CK:n], snew[0:r, b, :], st[0:r, 3:4]))
                    vec.tensor_tensor(st[0:r, 0:1], st[0:r, 1:2], st[0:r, 3:4], ALU.min).then_inc(masked, 1)

            def normalise(u):
                r, n = span(ATT[u])
                st = att[:, 4 * (u % SR):4 * (u % SR) + 4]
                dve.wait_ge(exped, u + 1)
                then(vec.reciprocal(st[0:r, 3:4], st[0:r, 2:3]))
                vec.tensor_scalar(score[u % SR][0:r, 0:n], score[u % SR][0:r, 0:n], st[0:r, 3:4], None,
                                  ALU.mult).then_inc(normed, 1)

            def store_heads(u):
                unit = ATT[u]
                dve.wait_ge(pv_done, u + 1)
                out = half(6 + u % 2)
                if unit[0] != "s":
                    h, t = unit
                    r0 = HD * (h % 2)
                    vec.tensor_copy(featT[r0:r0 + HD, 2 + h // 2, t * P:(t + 1) * P],
                                    out[r0:r0 + HD, 0:P]).then_inc(att_ready, 1)
                else:
                    b = unit[1]
                    o3 = out[:, 0:PAIRS * 8].rearrange("p (r c) -> p r c", c=8)
                    for s in range(2):
                        ins = vec.tensor_copy(featT[HD * s:HD * s + HD, 2:2 + PAIRS, SEQ + NS * b:SEQ + NS * b + NS],
                                              o3[HD * s:HD * s + HD, :, NS * s:NS * s + NS])
                    ins.then_inc(att_ready, 1)

            for u in range(len(ATT) + 4):
                if u < len(ATT):
                    mask_max(u)
                if 1 <= u <= len(ATT):
                    normalise(u - 1)
                if u >= 4:
                    store_heads(u - 4)

            dve.wait_ge(x_again, 16 * NT)
            dve.wait_ge(gain_in, 32)

            def norm_x2(t):
                n = TILES[t][1]
                dve.wait_ge(squared2, t + 1)
                scaled_norm(t, xn[0:n, t, :], x[0:n, t, :]).then_inc(xn_ready, 1)

            for t in range(NT + 1):
                if t < NT:
                    n = TILES[t][1]
                    dve.wait_ge(out_done, t + 1)
                    vec.tensor_tensor(x[0:n, t, :], x[0:n, t, :], wide(t % 2, D)[0:n], ALU.add).then_inc(x2_ready, 1)
                if t >= 1:
                    norm_x2(t - 1)

            def route(t, h, k, link):
                n = TILES[t][1]
                sc = [s_cur[0:n, c, :] for c in range(2)]
                sl = [s_left[0:n, c, :] for c in range(2)]
                wait_apart(dve, s_ready, k + 1)
                for c in range(2):
                    ins = vec.max(val[c][0:n, 0:8], sc[c])
                link(ins)
                for c in range(2):
                    vec.max_index(idx[c][0:n, 0:8], val[c][0:n, 0:8], sc[c])
                    ins = vec.match_replace(sl[c], val[c][0:n, 0:8], sc[c], -3e38)
                link(ins)
                for c in range(2):
                    ins = vec.max(val[c][0:n, 8:16], sl[c])
                link(ins)
                vec.tensor_tensor(cand[0:n, :].rearrange("p (i j) -> p i j", i=TOPK),
                                  val[0][0:n, :].unsqueeze(2).to_broadcast([n, TOPK, TOPK]),
                                  val[1][0:n, :].unsqueeze(1).to_broadcast([n, TOPK, TOPK]), ALU.add)
                for c in range(2):
                    ins = vec.max_index(idx[c][0:n, 8:16], val[c][0:n, 8:16], sl[c])
                link(ins)
                vec.max(top[0:n, 0:8], cand[0:n, :])
                for c in range(2):
                    ins = vec.tensor_copy(idf[c][0:n, :], idx[c][0:n, :])
                link(ins)
                vec.max_index(pos[0:n, 0:8], top[0:n, 0:8], cand[0:n, :])
                ins = vec.match_replace(cand_left[0:n, :], top[0:n, 0:8], cand[0:n, :], -3e38)
                link(ins)
                ins = vec.max(top[0:n, 8:16], cand_left[0:n, :])
                link(ins)
                vec.max_index(pos[0:n, 8:16], top[0:n, 8:16], cand_left[0:n, :])
                ins = vec.tensor_scalar(tops[0:n, bass.ds(h, 1), :].rearrange("p o k -> p (o k)"), top[0:n, :], top[0:n, 0:1],
                                  None, ALU.subtract)
                link(ins)
                vec.tensor_scalar(digit[0][0:n, :], pos[0:n, :], 4, None, ALU.logical_shift_right)
                ins = vec.tensor_scalar(digit[1][0:n, :], pos[0:n, :], TOPK - 1, None, ALU.bitwise_and)
                link(ins)
                for c in range(2):
                    ins = vec.tensor_tensor(hot[c][0:n], digit[c][0:n, :].unsqueeze(2).to_broadcast([n, TOPK, TOPK]),
                                      iota[0:n, :].unsqueeze(1).to_broadcast([n, TOPK, TOPK]), ALU.is_equal)
                link(ins)
                for c in range(2):
                    ins = vec.tensor_tensor(hot[c][0:n], hot[c][0:n], idf[c][0:n, :].unsqueeze(1).to_broadcast([n, TOPK, TOPK]),
                                      ALU.mult)
                link(ins)
                for c in range(2):
                    ins = vec.tensor_reduce(pick[c][0:n, :], hot[c][0:n], AX.X, ALU.add)
                link(ins)
                ins = vec.tensor_scalar(eidf[0:n, :], pick[0][0:n, :], float(NKEYS), None, ALU.mult)
                link(ins)
                dst = (eid[0:n, bass.ds(k * TOPK, TOPK)] if t < SAMP
                       else eid_samp[0:n, bass.ds(h * TOPK, TOPK)])
                vec.tensor_tensor(dst, eidf[0:n, :], pick[1][0:n, :], ALU.add).then_inc(
                    eid_ready if t < SAMP else eid_samp_ready, 1)

            def linker(start):
                done = [0]

                def link(ins):
                    done[0] += 1
                    ins.then_inc(route_link, 1)
                    wait_apart(dve, route_link, start + done[0])
                return link

            def finish_gates(t):
                n = TILES[t][1]
                dve.wait_ge(tops_exped, t + 1)
                g3 = (gate[0:n, FIRST[t] * TOPK:(FIRST[t] + HEADS) * TOPK] if t < SAMP
                      else gate_samp[0:n, :]).rearrange("p (h k) -> p h k", h=HEADS)
                then(vec.tensor_reduce(den8[0:n, :], tops[0:n], AX.X, ALU.add))
                then(vec.reciprocal(rden8[0:n, :], den8[0:n, :]))
                then(vec.tensor_tensor(g3, tops[0:n], rden8[0:n, :].unsqueeze(2).to_broadcast([n, HEADS, TOPK]), ALU.mult))
                if t == SAMP:
                    a, m = FIRST[t] * TOPK, SLOTS // GROUPS
                    dve.wait_ge(eid_samp_ready, HEADS)
                    for g in range(GROUPS):
                        ins = vec.tensor_copy(eid[g * NSAMP:(g + 1) * NSAMP, a:a + m],
                                              eid_samp[0:NSAMP, g * m:(g + 1) * m])
                    ins.then_inc(eid_ready, STEPS[SAMP])
                    for g in range(GROUPS):
                        ins = vec.tensor_copy(gate[g * NSAMP:(g + 1) * NSAMP, a:a + m], gate_samp[0:NSAMP, g * m:(g + 1) * m])
                    then(ins)

            def finish_y(t):
                n = TILES[t][1]
                s = rstd[0:n, t:t + 1]
                dve.wait_ge(y_squared, t + 1)
                then(vec.reciprocal(s, rms[0:n, t:t + 1]))
                vec.scalar_tensor_tensor(out=x[0:n, t, :], in0=x[0:n, t, :], scalar=s, in1=gain[0:n, :],
                                         op0=ALU.mult, op1=ALU.mult).then_inc(y_ready, 1)

            def set_x(t):
                if t < SAMP:
                    ins = vec.tensor_copy(x_cur, xn[:, t, :])
                else:
                    for g in range(GROUPS):
                        ins = vec.tensor_copy(x_cur[g * NSAMP:(g + 1) * NSAMP, :], xn[0:NSAMP, t, :])
                return ins

            def step(t, g, h, route_tile):
                for j in range(TOPK):
                    s = j % UR
                    dve.wait_ge(u_landed[s], (g * (TOPK // UR) + j // UR + 1) * 16)
                    ins = vec.tensor_tensor_reduce(out=u_ring[s], in0=u_ring[s], in1=x_cur, scale=1.0, scalar=0.0,
                                                   op0=ALU.mult, op1=ALU.add, accum_out=hid[:, j:j + 1])
                    ins.then_inc(u_free, 1)
                dve.wait_ge(gelu_done, g + 1)
                vec.tensor_tensor(wts[:], gelu[:], gate[:, bass.ds(g * TOPK, TOPK)], ALU.mult).then_inc(w_ready, 1)
                if route_tile is not None:
                    k = g + HEADS
                    route(route_tile, h, k, linker(k * LINKS))

            dve.wait_ge(xn_turned, NT)
            dve.wait_ge(xnT_ready, NT)
            for h in range(HEADS):
                route(0, h, h, linker(h * LINKS))
            ins = set_x(0)
            ins.then_inc(u_free, UR)
            dve.wait_ge(u_free, UR)
            finish_gates(0)
            for t in range(NT):
                last = STEPS[t] - 1
                with dve.Fori(0, last) as i:
                    step(t, i + FIRST[t], i, t + 1 if t < SAMP else None)
                step(t, last + FIRST[t], last, t + 1 if t < SAMP else None)
                if t < SAMP:
                    then(set_x(t + 1))
                if t == 1:
                    dve.wait_ge(gain_in, 48)
                if t >= 1:
                    finish_y(t - 1)
                if t < SAMP:
                    finish_gates(t + 1)
            finish_y(SAMP)

        @block.gpsimd
        def _(pool):
            pool.wait_ge(kv_out, 16 * (3 * NT + 1))
            pool.wait_ge(qkT_ready, len(QK))
            for s in range(2):
                nc.gpsimd.memset(q_blk[s], 0.0).then_inc(qz, 1)
            pool.wait_ge(qz, 2)
            for b in range(NB):
                if b >= 2:
                    pool.wait_ge(scored, samp_at[b - 2] + 1)
                for s in range(2):
                    dst = blocks_of(q_blk[b % 2], HD * s, NS * s)
                    ins = nc.gpsimd.tensor_copy(dst, qT[HD * s:HD * s + HD, :, SEQ + NS * b:SEQ + NS * b + NS])
                ins.then_inc(qb_ready, 1)

            def gather(ring, indices, s, table, column, landed, n_staged):
                nc.gpsimd.tensor_copy(indices[:, s:s + 1], eid[:, bass.ds(column, 1)]).then_inc(staged, 1)
                wait_apart(pool, staged, n_staged)
                nc.gpsimd.indirect_dma_start(
                    out=ring[s], out_offset=None, in_=table,
                    in_offset=bass.IndirectOffsetOnAxis(ap=indices[:, s:s + 1], axis=0)).then_inc(landed[s], 16)

            pool.wait_ge(eid_ready, 1)
            for j in range(TOPK):
                pool.wait_ge(u_free, j + 1)
                gather(u_ring, u_idx, j % UR, u_tab, j, u_landed, j + 1)

            def step(g, more):
                if more:
                    wait_apart(pool, eid_ready, g + 2)
                for j in range(TOPK):
                    before = (g * 2 + 1) * TOPK + (2 * j if more else j)
                    if more:
                        wait_apart(pool, u_free, (g + 1) * TOPK + j + 1)
                        gather(u_ring, u_idx, j % UR, u_tab, (g + 1) * TOPK + j, u_landed, before + 1)
                    wait_apart(pool, v_free, g * TOPK + j + 1)
                    gather(v_ring, v_idx, j % VR, v_tab, g * TOPK + j, v_landed, before + (2 if more else 1))

            with pool.Fori(0, NSTEP - 1) as g:
                step(g, True)
            step(NSTEP - 1, False)


def counts_log(dist, reach):
    c = sum(((dist >= 0) & (dist <= w // d * d) & (dist % d == 0) & reach).astype(np.int64) for w, d in BRANCHES)
    return np.where(c > 0, np.log(np.maximum(c, 1)), NEG).astype(np.float32)


def shape_tables():
    r = np.arange(P)
    ident = np.eye(P, dtype=np.float32)
    logc = counts_log(r[:, None] - np.arange(512)[None, :] + 384, True)
    m = np.arange(STRIDED)
    first = 16 * (m // NS) + m % NS
    near = np.arange(PAST - NEAR, PAST)
    rest = np.setdiff1d(np.arange(PAST), np.concatenate([first, near]))
    order = np.concatenate([first, near, rest])
    q = np.tile(np.arange(NS), NH)
    smask = counts_log(PAST + q[:, None] - order[None, :CK], True)
    new_b, new_j = np.arange(NEWK) // NS, np.arange(NEWK) % NS
    snew = np.stack([counts_log(q[:, None] - new_j[None, :], new_b[None, :] == b) for b in range(NB)], axis=1)
    pos = np.concatenate([np.arange(SEQ), PAST + np.tile(np.arange(NS), NB)]).astype(np.float32)
    rot = HD // 4
    inv = np.float32(500000.0) ** (-np.arange(0, rot, 2, dtype=np.float32) / np.float32(rot))
    ang = pos[:, None] * inv[None, :].astype(np.float32)
    c, s = np.cos(ang), np.sin(ang)
    rope = np.concatenate([c, c, -s, s], axis=1).astype(np.float32)
    iota = np.tile(np.arange(TOPK, dtype=np.float32), (P, 1))
    tril = (r[:, None] <= r[None, :]).astype(np.float32)
    b, i = np.arange(NSAMP) // NS, np.arange(NSAMP) % NS
    blockm = ((b[:, None] == b[None, :]) & (i[:, None] <= i[None, :])).astype(np.float32)
    return order, dict(ident_c=ident, logc_c=logc, smask_c=smask, snew_c=snew, rope_c=rope, iota_c=iota,
                       tril_c=tril, blockm_c=blockm)


def kernel(x_prompt, x_sample, cache_k_win, cache_v_win, attn_norm, w_in, ln_v_g, ln_v_b, w_s, b_s, w_out,
           ffn_norm, peer_w_q, peer_sub_keys, peer_u, peer_v, final_norm):
    import concourse.bacc as bacc
    from concourse.bass_utils import run_bass_kernel_spmd

    f = np.asarray
    order, tables = shape_tables()
    arrays = dict(
        x_p=f(x_prompt)[0], x_s=f(x_sample).reshape(NSAMP, D),
        k_cache=f(cache_k_win)[0].reshape(NB, PAST, DB)[:, order].transpose(0, 2, 1),
        v_cache=f(cache_v_win)[0].reshape(NB, PAST, DB)[:, order],
        gains=np.stack([f(attn_norm)[0], f(ffn_norm)[0], f(final_norm)]),
        w_in=f(w_in)[0], ln_gb=np.stack([f(ln_v_g)[0], f(ln_v_b)[0]]),
        w_sT=f(w_s)[0].transpose(0, 2, 1), b_sT=f(b_s)[0].T, w_out=f(w_out)[0], w_q=f(peer_w_q)[0],
        keysT=f(peer_sub_keys)[0].reshape(2 * HEADS * NKEYS, P).T, u_tab=f(peer_u)[0], v_tab=f(peer_v)[0],
        **tables)
    outs = dict(y_p=(SEQ, D), y_s=(NSAMP, D), k_p=(SEQ, DB), v_p=(SEQ, DB), k_s=(NSAMP, DB), v_s=(NSAMP, DB),
                gv_s=(NSAMP, DA))
    nc = bacc.Bacc("TRN2", target_bir_lowering=False, num_devices=1)
    aps, feeds = {}, {}
    for name, a in arrays.items():
        a = np.ascontiguousarray(a)
        feeds["in_" + name] = a
        aps[name] = nc.dram_tensor("in_" + name, a.shape, mybir.dt.from_np(a.dtype), kind="ExternalInput").ap()
    for name, shape in outs.items():
        aps[name] = nc.dram_tensor("out_" + name, shape, F32, kind="ExternalOutput").ap()
    build(nc, **aps)
    got = run_bass_kernel_spmd(nc, [feeds], core_ids=[0]).results[0]
    y_p, y_s, k_p, v_p, k_s, v_s, gv_s = (got["out_" + name] for name in outs)
    return (y_p.reshape(1, SEQ, D), y_s.reshape(NB, NS, D),
            k_p.reshape(1, 1, SEQ, NH, HD), v_p.reshape(1, 1, SEQ, NH, HD),
            k_s.reshape(1, NB, NS, NH, HD), v_s.reshape(1, NB, NS, NH, HD), gv_s.reshape(1, NB, NS, DA))
```

```python
import math
from contextlib import ExitStack

import numpy as np

import concourse.bass as bass
from concourse import mybir
from concourse.alu_op_type import AluOpType as ALU

ACT = mybir.ActivationFunctionType
AX = mybir.AxisListType
F32 = mybir.dt.float32
U32 = mybir.dt.uint32

P = 128
D = 1024
KD = D // P
SEQ = 512
NB, NS = 8, 4
NSAMP = NB * NS
PAST = 1024
DA, DB, NH, HD = 256, 768, 12, 64
GA = 4
PAIRS = NH // 2
TOK = SEQ + NSAMP
TILES = [(t * P, P) for t in range(SEQ // P)] + [(SEQ, NSAMP)]
NT = len(TILES)
SAMP = NT - 1
HALF = DB // 2
CHUNKS = [("uv", 0, 2 * DA)] + [(n, 2 * DA + i * DB + j * HALF, HALF)
                                for i, n in enumerate("qkv") for j in range(2)]
BRANCHES = ((128, 1), (512, 4), (2048, 16))
NEG = -1e30
EPS = 1e-6
STRIDED = 128
NEAR = 512
CK = STRIDED + NEAR
NEWK = NSAMP
SROWS = NH * NS
SCOLS = CK + NEWK

HEADS = 8
NKEYS = 128
TOPK = 16
SLOTS = HEADS * TOPK
UR, VR = 8, 4
GROUPS = P // NSAMP
LINKS = 13
STEPS = [HEADS] * (NT - 1) + [HEADS // GROUPS]
FIRST = [sum(STEPS[:t]) for t in range(NT)]
NSTEP = sum(STEPS)


def build(nc, x_p, x_s, k_cache, v_cache, gains, w_in, ln_gb, w_sT, b_sT, w_out, w_q, keysT, u_tab, v_tab,
          ident_c, logc_c, smask_c, snew_c, rope_c, iota_c, tril_c, blockm_c,
          y_p, y_s, k_p, v_p, k_s, v_s, gv_s):
    ctx = ExitStack()
    with ctx:
        def sb(name, n, dt=F32):
            return ctx.enter_context(nc.sbuf_tensor(name, [P, n], dt))

        def sem(name):
            return ctx.enter_context(nc.semaphore(name))

        area_w = sb("area_w", 16384)
        area_r = sb("area_r", 14720)
        area_t = sb("area_t", KD * TOK)
        area_x = sb("area_x", NT * D)
        area_v = sb("area_v", 6400)
        area_c = sb("area_c", 2176)

        def cut(area, a, *dims):
            n = math.prod(dims)
            v = area[:, a:a + n]
            if len(dims) == 2:
                v = v.rearrange("p (a b) -> p a b", a=dims[0])
            if len(dims) == 3:
                v = v.rearrange("p (a b c) -> p a b c", a=dims[0], b=dims[1])
            return v

        W_SLOTS = 4
        w_ring = [cut(area_w, s * KD * 512, KD, 512) for s in range(W_SLOTS)]
        kc = [cut(area_w, (1 - s) * 2 * PAIRS * CK, PAIRS, CK) for s in range(2)]
        vc = [cut(area_w, ((1 - s) * 2 + 1) * PAIRS * CK, CK // P, DB) for s in range(2)]
        w_o = cut(area_w, KD * D, KD, D)
        WQ = KD * 2 * P
        wq = [cut(area_w, h * WQ, KD, 2 * P) for h in range(HEADS)]

        qT = cut(area_r, KD * D, PAIRS, TOK)
        kT = cut(area_r, KD * D + PAIRS * TOK, PAIRS, TOK)
        u_ring = [cut(area_r, s * D, D) for s in range(UR)]
        v_ring = [cut(area_r, (UR + s) * D, D) for s in range(VR)]
        keys = cut(area_r, (UR + VR) * D, 2 * HEADS * NKEYS)

        featT = cut(area_t, 0, KD, TOK)

        x = cut(area_x, 0, NT, D)
        SR = 4
        q_stage = [cut(area_x, s * HALF, HALF) for s in range(3)]
        k_stage = [cut(area_x, (3 + s) * HALF, HALF) for s in range(2 * NT)]
        score = [cut(area_x, s * SCOLS, SCOLS) for s in range(SR)]
        probT = [cut(area_x, SR * SCOLS + s * 512, 512) for s in range(2)]
        QB = 344
        q_blk = [cut(area_x, SR * SCOLS + 1024 + s * QB, QB) for s in range(2)]

        OTHERS, OROWS = 32, 32 + SROWS // 2
        o_stage = cut(area_x, SR * SCOLS + 1024 + 2 * QB, HALF)

        def blocks_of(q, r0, c0):
            w = SROWS + 2 * NS
            v = q[r0:r0 + HD, 0:PAIRS * w + 2 * NS]
            return v[:, c0:c0 + PAIRS * w].rearrange("p (r w) -> p r w", w=w)[:, :, 0:NS]


        h_stage = [cut(area_v, s * D, D) for s in range(2)]
        v_tok = cut(area_v, 0, NT, DB)
        u_tok = cut(area_v, NT * DB, NT, DA)
        vn = cut(area_v, NT * (DB + DA), NT, DA)
        xn = cut(area_v, 0, NT, D)

        logc = cut(area_c, 0, 512)
        smask = cut(area_c, 512, CK)
        snew = cut(area_c, 512 + CK, NB, NEWK)
        lngb = cut(area_c, 512 + CK + NB * NEWK, 2, DA)

        gain = sb("gain", D)
        ident = sb("ident", P)
        w_s = sb("w_s", GA * P)
        w_s32 = sb("w_s32", GA * NS)
        w_sb = sb("w_sb", GA * NSAMP)
        bs = sb("bs", 2 * GA)
        tril = sb("tril", P)
        blockm = sb("blockm", NSAMP)
        rope = sb("rope", NT * 32)
        rope_ab = sb("rope_ab", 4 * 96)
        iota = sb("iota", TOPK)
        small = sb("small", 24)
        eps = sb("eps", 1)
        lnst = sb("lnst", NT * 8)
        att = sb("att", SR * 4)

        eid = sb("eid", NSTEP * TOPK, U32)
        gate = sb("gate", NSTEP * TOPK)
        u_idx = sb("u_idx", UR, U32)
        v_idx = sb("v_idx", VR, U32)
        hid = sb("hid", TOPK)
        gelu = sb("gelu", TOPK)
        wts = sb("wts", TOPK)
        ident4 = sb("ident4", NSAMP)

        diag = [cut(area_c, s * P, P) for s in range(VR)]
        q_row = cut(area_c, 512, 2 * P)
        q_col = cut(area_c, 768, 2, P)
        s_cur = [cut(area_v, NT * D + a, 2, NKEYS) for a in (0, 1024)]
        s_left = cut(area_v, NT * D + 256, 2, NKEYS)
        cand = cut(area_c, 1024, TOPK * TOPK)
        cand_left = cut(area_c, 1280, TOPK * TOPK)
        hot = [cut(area_v, NT * D + 512 + c * 256, TOPK, TOPK) for c in range(2)]
        tops = cut(area_c, 1536, HEADS, TOPK)
        eid_samp = cut(area_c, 1664, SLOTS)
        gate_samp = cut(area_c, 1792, SLOTS)
        rt = cut(area_c, 1920, 9 * TOPK)
        rtu = sb("rtu", 5 * TOPK, U32)
        val = [rt[:, c * TOPK:(c + 1) * TOPK] for c in range(2)]
        idf = [rt[:, (2 + c) * TOPK:(3 + c) * TOPK] for c in range(2)]
        pick = [rt[:, (4 + c) * TOPK:(5 + c) * TOPK] for c in range(2)]
        top = rt[:, 6 * TOPK:7 * TOPK]
        den8 = rt[:, 7 * TOPK:7 * TOPK + 8]
        rden8 = rt[:, 7 * TOPK + 8:8 * TOPK]
        eidf = rt[:, 8 * TOPK:9 * TOPK]
        idx = [rtu[:, c * TOPK:(c + 1) * TOPK] for c in range(2)]
        pos = rtu[:, 2 * TOPK:3 * TOPK]
        digit = [rtu[:, (3 + c) * TOPK:(4 + c) * TOPK] for c in range(2)]

        bank = [ctx.enter_context(nc.psum_tensor(f"bank{i}", [P, 2, 512], F32)) for i in range(4)]

        def half(i):
            return bank[i // 2][:, i % 2, :]

        def wide(i, n):
            return bank[i].rearrange("p a b -> p (a b)")[:, 0:n]

        acc = bank[0]
        x_cur = wide(1, D)
        ps_q, ps_qT, ps_s = half(4), half(5), half(6)

        x_in = [sem(f"x_in{t}") for t in range(NT)]
        ident_in, consts_in, gain_in = sem("ident_in"), sem("consts_in"), sem("gain_in")
        w_in_sem = [sem(f"w_in{s}") for s in range(W_SLOTS)]
        w_out_in, keys_in = sem("w_out_in"), sem("keys_in")
        wq_in = [sem(f"wq_in{h}") for h in range(HEADS)]
        kc_in = [sem(f"kc_in{s}") for s in range(2)]
        vc_in = [sem(f"vc_in{s}") for s in range(2)]
        kv_out, y_out = sem("kv_out"), sem("y_out")
        dv = sem("dv")
        eps_set, summed, ln_stats, ln_root = sem("eps_set"), sem("summed"), sem("ln_stats"), sem("ln_root")
        squared, h_ready, h_turned, hT_ready = sem("squared"), sem("h_ready"), sem("h_turned"), sem("hT_ready")
        proj_done, uv_read, qkv_read = sem("proj_done"), sem("uv_read"), sem("qkv_read")
        roped, qk_turned, qkT_ready = sem("roped"), sem("qk_turned"), sem("qkT_ready")
        ws_ready, mixed_done, gated, g_turned, gT_ready = (sem("ws_ready"), sem("mixed_done"), sem("gated"),
                                                           sem("g_turned"), sem("gT_ready"))
        qb_ready, scored, masked, exped, normed = (sem("qb_ready"), sem("scored"), sem("masked"), sem("exped"),
                                                   sem("normed"))
        p_turned, pT_ready, pv_done, att_ready = sem("p_turned"), sem("pT_ready"), sem("pv_done"), sem("att_ready")
        o_copied, o_turned = sem("o_copied"), sem("o_turned")
        out_done, x2_ready, squared2, xn_ready = sem("out_done"), sem("x2_ready"), sem("squared2"), sem("xn_ready")
        xn_turned, xnT_ready = sem("xn_turned"), sem("xnT_ready")
        qz = sem("qz")
        q_done, q_copied, q_turned, qT_copied = sem("q_done"), sem("q_copied"), sem("q_turned"), sem("qT_copied")
        s_done, s_ready = sem("s_done"), sem("s_ready")
        tops_exped = sem("tops_exped")
        u_landed = [sem(f"u_landed{s}") for s in range(UR)]
        v_landed = [sem(f"v_landed{s}") for s in range(VR)]
        u_free, v_free = sem("u_free"), sem("v_free")
        staged = sem("staged")
        gelu_done, w_ready, diag_ready = sem("gelu_done"), sem("w_ready"), sem("diag_ready")
        passed = sem("passed")
        samp_gates = sem("samp_gates")
        eid_ready, eid_samp_ready = sem("eid_ready"), sem("eid_samp_ready")
        route_link = sem("route_link")
        acc_read, y_squared, y_ready = sem("acc_read"), sem("y_squared"), sem("y_ready")

        block = ctx.enter_context(nc.Block())

        N_CONST = 1 + NT + 1 + 2 * NB + 7 + GROUPS
        UNITS = [(c, t) for c in range(len(CHUNKS)) for t in range(NT)]
        QK = [(c, t) for c, t in UNITS if CHUNKS[c][0] in "qk"]
        qk_at = {u: i for i, u in enumerate(QK)}
        N_QKV = len(UNITS) - NT
        ATT = []
        for i in range(NH * (NT - 1)):
            ATT.append((i // (NT - 1), i % (NT - 1)))
            if i % 6 == 5:
                ATT.append(("s", i // 6))
        samp_at = {b: ATT.index(("s", b)) for b in range(NB)}
        NOUT = 2 * 2 * NT
        MIXED = NT

        AHEAD = HEADS + 1
        N_ROUTED = HEADS * NT

        def routed_in(g):
            ks = (2 * g + 2, 2 * g + 3) if g < HEADS - 1 else (g + AHEAD,)
            return [k for k in ks if k < N_ROUTED]

        def scored_in(g):
            return [(k // HEADS, k % HEADS, k) for k in routed_in(g + 1)]

        def steps_of(t):
            loop = STEPS[t] - 2 if t > 0 else 0
            return loop, range(FIRST[t] + loop, FIRST[t] + STEPS[t])

        def gates_in(g):
            if g < HEADS // 2:
                return [(0, 2 * g, 2 * g + 2)]
            if g % HEADS == HEADS - 1 and g // HEADS < SAMP:
                return [(g // HEADS + 1, 0, HEADS)]
            return []

        def s_buf(k):
            return k % 2 if isinstance(k, int) and k < 2 * HEADS else 0

        def g_is(g, number):
            return isinstance(g, int) and g == number

        def beside(g):
            return (3, 5) if g_is(g, 0) else (0, 2)

        def span(u):
            return (P, (u[1] + 1) * P) if u[0] != "s" else (SROWS, SCOLS)

        def wait_apart(engine, what, value):
            engine.wait_ge(what, value)
            engine.sem_inc(passed, 1)

        def peer_x(t):
            return NSAMP if t == SAMP else P

        @block.sync
        def _(sp):
            for t, (a, n) in enumerate(TILES):
                src = x_p[a:a + n, :] if t < SAMP else x_s
                sp.dma_start(x[0:n, t, :], src).then_inc(x_in[t], 16)
                if t == 0:
                    sp.dma_start(gain[:], gains[0:1, :].broadcast_to([P, D])).then_inc(gain_in, 16)
                    sp.dma_start(ident[:], ident_c).then_inc(ident_in, 16)

            def load_w(c):
                s = c % W_SLOTS
                _, a, n = CHUNKS[c]
                sp.dma_start(w_ring[s][:, :, 0:n],
                             w_in[:, a:a + n].rearrange("(k p) n -> p k n", p=P)).then_inc(w_in_sem[s], 16)

            load_w(0)
            load_w(1)
            load_w(2)
            load_w(3)
            for c in range(W_SLOTS, len(CHUNKS)):
                sp.wait_ge(proj_done, NT * (c - W_SLOTS + 1))
                load_w(c)
            sp.wait_ge(h_ready, NT)
            sp.dma_start(gain[:], gains[1:2, :].broadcast_to([P, D])).then_inc(gain_in, 16)
            for c, t in QK:
                if CHUNKS[c][0] == "k":
                    i, (a, n) = qk_at[c, t], TILES[t]
                    sp.wait_ge(roped, i + 1)
                    dst, a = (k_p, a) if t < SAMP else (k_s, 0)
                    j = CHUNKS[c][1] - 2 * DA - DB
                    sp.dma_start(dst[a:a + n, j:j + HALF], k_stage[i - 2 * NT][0:n, :]).then_inc(kv_out, 16)
            sp.wait_ge(qkv_read, N_QKV)
            for t, (a, n) in enumerate(TILES):
                dst, a = (v_p, a) if t < SAMP else (v_s, 0)
                sp.dma_start(dst[a:a + n, :], v_tok[0:n, t, :]).then_inc(kv_out, 16)
            sp.dma_start(gv_s, vn[0:NSAMP, SAMP, :]).then_inc(kv_out, 16)
            sp.wait_ge(proj_done, len(UNITS))
            for b in range(NB):
                s = b % 2
                if b >= 2:
                    sp.wait_ge(scored, samp_at[b - 2] + 1)
                sp.dma_start(kc[s], k_cache[b][:, 0:CK].rearrange("(r p) n -> p r n", p=P)).then_inc(kc_in[s], 16)
            sp.wait_ge(pv_done, samp_at[NB - 2] + 1)
            sp.dma_start(w_o, w_out.rearrange("(k p) n -> p k n", p=P)).then_inc(w_out_in, 16)
            sp.wait_ge(pv_done, len(ATT))
            sp.wait_ge(qb_ready, NB)
            sp.wait_ge(o_turned, NB)
            def load_x_again(t):
                a, n = TILES[t]
                src = x_p[a:a + n, :] if t < SAMP else x_s
                sp.dma_start(x[0:n, t, :], src).then_inc(x_in[t], 16)

            def load_wq(h):
                sp.dma_start(wq[h], w_q[:, 2 * P * h:2 * P * (h + 1)].rearrange("(k p) n -> p k n", p=P)).then_inc(
                    wq_in[h], 16)

            load_x_again(0)
            load_wq(0)
            load_x_again(1)
            load_wq(1)
            sp.dma_start(keys, keysT).then_inc(keys_in, 16)
            for t in range(2, NT):
                load_x_again(t)
            for h in range(2, HEADS // 2):
                load_wq(h)
            sp.wait_ge(out_done, 2 * NT)
            for h in range(HEADS // 2, HEADS):
                load_wq(h)
            sp.wait_ge(xn_ready, NT)
            sp.dma_start(gain[:], gains[2:3, :].broadcast_to([P, D])).then_inc(gain_in, 16)
            for t, (a, n) in enumerate(TILES):
                sp.wait_ge(y_ready, t + 1)
                dst = y_p[a:a + n, :] if t < SAMP else y_s
                sp.dma_start(dst, x[0:n, t, :]).then_inc(y_out, 16)
            sp.wait_ge(y_out, 16 * NT)
            sp.wait_ge(kv_out, 16 * (2 * NT + NT + 1))

        @block.tensor
        def _(pe):
            pe.wait_ge(ident_in, 16)

            def turn(out, src, n):
                return pe.transpose(out, src, ident[0:n, 0:n])

            for t, (a, n) in enumerate(TILES):
                pe.wait_ge(h_ready, t + 1)
                if t >= 2:
                    pe.wait_ge(hT_ready, t - 1)
                dst = bank[2 + t % 2]
                for k in range(KD):
                    mm = turn(dst[:, k // 4, (k % 4) * P:(k % 4) * P + n], h_stage[t % 2][0:n, k * P:(k + 1) * P], n)
                mm.then_inc(h_turned, 1)

            def turn_qk(i):
                c, t = QK[i]
                n = TILES[t][1]
                pe.wait_ge(roped, i + 1)
                if i >= 2:
                    pe.wait_ge(qkT_ready, i - 1)
                else:
                    pe.wait_ge(hT_ready, NT)
                src = q_stage[i % 3] if CHUNKS[c][0] == "q" else k_stage[i - 2 * NT]
                for j in range(3):
                    mm = turn(half(4 + i % 2)[:, j * P:j * P + n], src[0:n, j * P:(j + 1) * P], n)
                mm.then_inc(qk_turned, 1)

            for u, (c, t) in enumerate(UNITS):
                a, n = TILES[t]
                w = CHUNKS[c][2]
                if t == 0:
                    pe.wait_ge(w_in_sem[c % W_SLOTS], 16 * (c // W_SLOTS + 1))
                if c == 0:
                    pe.wait_ge(hT_ready, t + 1)
                if 3 <= u < NT + 3:
                    pe.wait_ge(uv_read, u - 2)
                elif u >= NT + 3:
                    pe.wait_ge(qkv_read, u - 2 - NT)
                for k in range(KD):
                    mm = pe.matmul(half(u % 3)[0:n, 0:w], featT[:, k, a:a + n], w_ring[c % W_SLOTS][:, k, 0:w],
                                   start=(k == 0), stop=(k == KD - 1))
                mm.then_inc(proj_done, 1)
                if u >= 2 and UNITS[u - 2] in qk_at:
                    turn_qk(qk_at[UNITS[u - 2]])

            pe.wait_ge(ws_ready, 1)
            pe.wait_ge(qkT_ready, len(QK))

            def gmlp(t):
                n = TILES[t][1]
                if t >= 2:
                    pe.wait_ge(gated, t - 1)
                for g in range(GA):
                    lhs = w_s[:, g * P:(g + 1) * P] if t < SAMP else w_sb[0:n, g * NSAMP:(g + 1) * NSAMP]
                    mm = pe.matmul(half(4 + t % 2)[0:n, g * HD:(g + 1) * HD], lhs, vn[0:n, t, g * HD:(g + 1) * HD],
                                   start=True, stop=True)
                mm.then_inc(mixed_done, 1)

            def turn_gated(t):
                n = TILES[t][1]
                pe.wait_ge(gated, t + 1)
                if t >= 2:
                    pe.wait_ge(gT_ready, t - 1)
                for k in range(2):
                    mm = turn(half(6 + t % 2)[:, k * P:k * P + n], u_tok[0:n, t, k * P:(k + 1) * P], n)
                mm.then_inc(g_turned, 1)

            for t in range(MIXED + 1):
                if t < MIXED:
                    gmlp(t)
                if t >= 1:
                    turn_gated(t - 1)
            pe.wait_ge(gT_ready, NT)
            pe.wait_ge(qkv_read, N_QKV)

            def scores(u):
                unit = ATT[u]
                if u >= 2:
                    pe.wait_ge(masked, u - 1)
                if unit[0] != "s":
                    h, t = unit
                    r0, pr = HD * (h % 2), h // 2
                    n = (t + 1) * P
                    mm = pe.matmul(wide(u % 2, n), qT[r0:r0 + HD, pr, t * P:(t + 1) * P], kT[r0:r0 + HD, pr, 0:n],
                                   start=True, stop=True)
                else:
                    b = unit[1]
                    pe.wait_ge(qb_ready, b + 1)
                    pe.wait_ge(kc_in[b % 2], 16 * (b // 2 + 1))
                    for lo, hi, src in ((0, 512, kc[b % 2][:, :, 0:512]), (512, CK, kc[b % 2][:, :, 512:CK]),
                                        (CK, SCOLS, kT[:, :, SEQ:TOK])):
                        for pr in range(PAIRS):
                            mm = pe.matmul(wide(u % 2, D)[0:SROWS, lo:hi], q_blk[b % 2][:, pr * SROWS:(pr + 1) * SROWS],
                                           src[:, pr, :], start=(pr == 0), stop=(pr == PAIRS - 1))
                mm.then_inc(scored, 1)

            def turn_probs(u):
                r, n = span(ATT[u])
                pe.wait_ge(normed, u + 1)
                if u >= 2:
                    pe.wait_ge(pT_ready, u - 1)
                for j, a in enumerate(range(0, n, P)):
                    w = min(P, n - a)
                    mm = turn(half(4 + u % 2)[0:w, j * r:(j + 1) * r], score[u % SR][0:r, a:a + w], r)
                mm.then_inc(p_turned, 1)

            def outputs(u):
                unit = ATT[u]
                out = half(6 + u % 2)
                pe.wait_ge(pT_ready, u + 1)
                if u >= 2:
                    pe.wait_ge(att_ready, u - 1)
                if unit[0] != "s":
                    h, t = unit
                    r0 = HD * (h % 2)
                    for j in range(t + 1):
                        mm = pe.matmul(out[r0:r0 + HD, 0:P], v_tok[:, j, h * HD:(h + 1) * HD],
                                       probT[u % 2][:, j * P:(j + 1) * P], start=(j == 0), stop=(j == t))
                else:
                    b = unit[1]
                    pe.wait_ge(vc_in[b % 2], 16 * (b // 2 + 1))
                    for f, rows, base in ((0, OTHERS, 0), (1, SROWS // 2, OTHERS)):
                        for j in range(CK // P + 1):
                            new = j == CK // P
                            nk, a = (NEWK if new else P), j * SROWS + f * (SROWS // 2)
                            v = v_tok[0:NEWK, SAMP] if new else vc[b % 2][:, j]
                            mm = pe.matmul(out[base:base + rows, 0:HALF], probT[u % 2][0:nk, a:a + rows],
                                           v[:, f * HALF:(f + 1) * HALF], start=(j == 0), stop=new)
                mm.then_inc(pv_done, 1)

            def turn_outputs(u):
                pe.wait_ge(o_copied, ATT[u][1] + 1)
                for c in range(PAIRS // 2):
                    mm = turn(half(6 + u % 2)[:, c * OROWS:(c + 1) * OROWS], o_stage[0:OROWS, c * P:(c + 1) * P], OROWS)
                mm.then_inc(o_turned, 1)

            for u in range(len(ATT) + 4):
                if u < len(ATT):
                    scores(u)
                if 2 <= u < len(ATT) + 2:
                    turn_probs(u - 2)
                if 3 <= u < len(ATT) + 3:
                    outputs(u - 3)
                if u >= 4 and ATT[u - 4][0] == "s":
                    turn_outputs(u - 4)

            def project_out(t, c):
                a, n = TILES[t]
                v = 2 * t + c
                if v >= 2:
                    pe.wait_ge(x2_ready, v - 1)
                for k in range(KD):
                    mm = pe.matmul(half(c)[0:n, :], featT[:, k, a:a + n], w_o[:, k, c * 512:(c + 1) * 512],
                                   start=(k == 0), stop=(k == KD - 1))
                mm.then_inc(out_done, 1)

            def turn_xn(v):
                t, n = v // 2, TILES[v // 2][1]
                pe.wait_ge(xn_ready, t + 1)
                if v >= 1:
                    pe.wait_ge(xnT_ready, v)
                for k in range(4):
                    f = (v % 2 * 4 + k) * P
                    mm = turn(half(7)[:, k * P:k * P + n], xn[0:n, t, f:f + P], n)
                mm.then_inc(xn_turned, 1)

            def queries(t, h, n_done):
                a, n = TILES[t]
                if not isinstance(n_done, int) or n_done:
                    pe.wait_ge(q_copied, n_done)
                for k in range(KD):
                    mm = pe.matmul(ps_q[0:n, 0:2 * P], featT[:, k, a:a + n], area_w[:, bass.ds(h * WQ + k * 2 * P, 2 * P)],
                                   start=(k == 0), stop=(k == KD - 1))
                mm.then_inc(q_done, 1)

            def turn_queries(t, n_done):
                n = TILES[t][1]
                wait_apart(pe, q_copied, n_done + 1)
                if not isinstance(n_done, int) or n_done:
                    wait_apart(pe, qT_copied, n_done)
                for c in range(2):
                    mm = turn(ps_qT[:, c * P:c * P + n], q_row[0:n, c * P:(c + 1) * P], n)
                mm.then_inc(q_turned, 1)

            def key_scores(t, h, n_done):
                n = TILES[t][1]
                pe.wait_ge(qT_copied, n_done + 1)
                if not isinstance(n_done, int) or n_done:
                    pe.wait_ge(s_ready, n_done)
                for c in range(2):
                    mm = pe.matmul(ps_s[0:n, c * NKEYS:(c + 1) * NKEYS], q_col[:, c, 0:n],
                                   keys[:, bass.ds((2 * h + c) * NKEYS, NKEYS)], start=True, stop=True)
                mm.then_inc(s_done, 1)

            def slot(t, g, j):
                n = peer_x(t)
                s = j % VR
                pe.wait_ge(diag_ready, g * TOPK + j + 1)
                pe.wait_ge(v_landed[s], (g * (TOPK // VR) + j // VR + 1) * 16)
                for c in range(2):
                    mm = pe.matmul(acc[0:n, c, :], diag[s][:, 0:n], v_ring[s][:, c * 512:(c + 1) * 512],
                                   start=False, stop=False, skip_group_check=True)
                mm.then_inc(v_free, 1)

            def step(t, g, nxt):
                for j in range(TOPK):
                    slot(t, g, j)
                    if g_is(g, 0) and j in (0, 2):
                        score_head(2 + j // 2)
                    if g_is(g, 1) and j % 2 == 0:
                        turn_xn(2 + j // 2)
                    for a, (tn, h, k) in zip(beside(g), nxt):
                        if isinstance(k, int) and k < HEADS and j == a:
                            pe.wait_ge(wq_in[h], 16)
                        if j == a:
                            queries(tn, h, k)
                        if j == a + 4:
                            turn_queries(tn, k)
                        if j == a + 8:
                            key_scores(tn, h, k)

            def score_head(k):
                pe.wait_ge(wq_in[k], 16)
                queries(0, k, k)
                turn_queries(0, k)
                if k == 0:
                    pe.wait_ge(keys_in, 16)
                key_scores(0, k, k)

            def start_sum(t):
                n = TILES[t][1]
                for c in range(2):
                    mm = pe.matmul(acc[0:n, c, :], ident[0:n, 0:n], x[0:n, t, c * 512:(c + 1) * 512],
                                   start=True, stop=False, skip_group_check=True)
                return mm

            pe.wait_ge(w_out_in, 16)
            pe.wait_ge(att_ready, len(ATT))
            pe.wait_ge(masked, len(ATT))
            project_out(0, 0)
            project_out(0, 1)
            project_out(1, 0)
            turn_xn(0)
            turn_xn(1)
            pe.wait_ge(xnT_ready, 2)
            score_head(0)
            score_head(1)
            for v in range(3, 2 * NT):
                project_out(v // 2, v % 2)
            pe.wait_ge(x2_ready, 2 * NT)
            start_sum(0)
            for t in range(NT):
                if t >= 1:
                    pe.wait_ge(acc_read, t)
                    start_sum(t)
                loop, rest = steps_of(t)
                if loop:
                    with pe.Fori(0, loop) as i:
                        step(t, i + FIRST[t], [(t + 1, i + 2, i + FIRST[t] + AHEAD + 1)])
                for g in rest:
                    step(t, g, scored_in(g))

        @block.scalar
        def _(act):
            def copy(out, src, scale=1.0):
                return nc.scalar.activation(out, src, ACT.Copy, scale=scale)

            ssq, rms = small[:, 0:8], small[:, 8:16]

            def root(t, summed, k, done):
                n = TILES[t][1]
                act.wait_ge(summed, k + 1)
                nc.scalar.activation(rms[0:n, t:t + 1], ssq[0:n, t:t + 1], ACT.Sqrt, scale=1.0 / D,
                                     bias=eps[0:n, :]).then_inc(done, 1)

            def square(t):
                n = TILES[t][1]
                act.wait_ge(x_in[t], 16)
                if t >= 2:
                    act.wait_ge(h_turned, t - 1)
                nc.scalar.activation(h_stage[t % 2][0:n, :], x[0:n, t, :], ACT.Square,
                                     accum_out=ssq[0:n, t:t + 1]).then_inc(summed, 1)
                root(t, summed, t, squared)

            def copy_turned(t):
                a, n = TILES[t]
                act.wait_ge(h_turned, t + 1)
                for c in range(2):
                    src = bank[2 + t % 2][:, c, :].rearrange("p (k n) -> p k n", k=4)[:, :, 0:n]
                    ins = copy(featT[:, 4 * c:4 * c + 4, a:a + n], src)
                ins.then_inc(hT_ready, 1)

            act.wait_ge(eps_set, 1)
            for t in range(NT + 1):
                if t < NT:
                    square(t)
                if t >= 1:
                    copy_turned(t - 1)

            def copy_qkT(i):
                c, t = QK[i]
                a, n = TILES[t]
                act.wait_ge(qk_turned, i + 1)
                dst = qT if CHUNKS[c][0] == "q" else kT
                b = (c - 1) % 2 * 3
                src = half(4 + i % 2)[:, 0:3 * P].rearrange("p (k n) -> p k n", k=3)[:, :, 0:n]
                copy(dst[:, b:b + 3, a:a + n], src).then_inc(qkT_ready, 1)

            for u, (c, t) in enumerate(UNITS):
                kind = CHUNKS[c][0]
                n = TILES[t][1]
                if kind == "uv":
                    st = lnst[0:n, 8 * t:8 * t + 8]
                    act.wait_ge(ln_stats, t + 1)
                    nc.scalar.activation(st[:, 5:6], st[:, 7:8], ACT.Sqrt, bias=eps[0:n, :]).then_inc(ln_root, 1)
                else:
                    act.wait_ge(proj_done, u + 1)
                    if kind == "v":
                        dst = v_tok[0:n, t, (c - 5) * HALF:(c - 4) * HALF]
                    else:
                        i = qk_at[c, t]
                        if kind == "q" and i >= 3:
                            act.wait_ge(qk_turned, i - 2)
                        dst = (q_stage[i % 3] if kind == "q" else k_stage[i - 2 * NT])[0:n, :]
                    copy(dst, half(u % 3)[0:n, 0:HALF], HD ** -0.5 if kind == "q" else 1.0).then_inc(qkv_read, 1)
                if u >= 2 and UNITS[u - 2] in qk_at:
                    copy_qkT(qk_at[UNITS[u - 2]])

            for t, (a, n) in enumerate(TILES):
                act.wait_ge(g_turned, t + 1)
                src = half(6 + t % 2)[:, 0:2 * P].rearrange("p (k n) -> p k n", k=2)[:, :, 0:n]
                copy(featT[:, 0:2, a:a + n], src).then_inc(gT_ready, 1)

            def exps(u):
                r, n = span(ATT[u])
                act.wait_ge(masked, u + 1)
                st = att[:, 4 * (u % SR):4 * (u % SR) + 4]
                nc.scalar.activation(score[u % SR][0:r, 0:n], score[u % SR][0:r, 0:n], ACT.Exp, bias=st[0:r, 0:1],
                                     scale=-1.0, accum_out=st[0:r, 2:3]).then_inc(exped, 1)

            def copy_pT(u):
                r, n = span(ATT[u])
                act.wait_ge(p_turned, u + 1)
                if u >= 2:
                    act.wait_ge(pv_done, u - 1)
                if ATT[u][0] != "s":
                    copy(probT[u % 2][:, 0:n], half(4 + u % 2)[:, 0:n]).then_inc(pT_ready, 1)
                else:
                    m = CK // P * SROWS
                    copy(probT[u % 2][:, 0:m], half(4 + u % 2)[:, 0:m])
                    copy(probT[u % 2][0:NEWK, m:m + SROWS], half(4 + u % 2)[0:NEWK, m:m + SROWS]).then_inc(pT_ready, 1)

            for u in range(len(ATT) + 2):
                if u < len(ATT):
                    exps(u)
                if u >= 2:
                    copy_pT(u - 2)

            act.wait_ge(pv_done, len(ATT))
            act.wait_ge(kv_out, 16 * (3 * NT + 1))
            def copy_xnT(v):
                a, n = TILES[v // 2]
                act.wait_ge(xn_turned, v + 1)
                c = v % 2 * 4
                src = half(7).rearrange("p (k n) -> p k n", k=4)[:, :, 0:n]
                copy(featT[:, c:c + 4, a:a + n], src).then_inc(xnT_ready, 1)

            def square_x2(t):
                n = TILES[t][1]
                act.wait_ge(x2_ready, 2 * t + 2)
                nc.scalar.activation(xn[0:n, t, :], x[0:n, t, :], ACT.Square,
                                     accum_out=ssq[0:n, t:t + 1]).then_inc(summed, 1)
                root(t, summed, NT + t, squared2)

            def copy_q(t, k):
                n = TILES[t][1]
                act.wait_ge(q_done, k + 1)
                if not isinstance(k, int) or k:
                    act.wait_ge(q_turned, k)
                copy(q_row[0:n, :], ps_q[0:n, 0:2 * P]).then_inc(q_copied, 1)

            def copy_qT(t, k):
                n = TILES[t][1]
                act.wait_ge(q_turned, k + 1)
                if not isinstance(k, int) or k:
                    act.wait_ge(s_done, k)
                copy(q_col[:, :, 0:n], ps_qT[:, 0:2 * P].rearrange("p (c n) -> p c n", c=2)[:, :, 0:n]).then_inc(qT_copied, 1)

            def copy_s(t, k):
                n = TILES[t][1]
                act.wait_ge(s_done, k + 1)
                if not isinstance(k, int) or k > 2 * HEADS:
                    act.wait_ge(route_link, (k - 1) * LINKS + 2)
                elif k >= 2:
                    act.wait_ge(route_link, (k - 2) * LINKS + 2)
                copy(s_cur[s_buf(k)][0:n], ps_s[0:n, 0:2 * NKEYS].rearrange("p (c n) -> p c n", c=2)).then_inc(s_ready, 1)

            def exp_tops(t, lo, hi):
                n = TILES[t][1]
                act.wait_ge(route_link, (t * HEADS + hi) * LINKS)
                nc.scalar.activation(tops[0:n, lo:hi], tops[0:n, lo:hi], ACT.Exp).then_inc(tops_exped, 1)

            def step(t, g, nxt):
                n = peer_x(t)
                act.wait_ge(u_free, UR + (g + 1) * TOPK)
                nc.scalar.activation(gelu[:], hid[:], ACT.Gelu).then_inc(gelu_done, 1)
                if g_is(g, 0):
                    square_x2(SAMP)
                act.wait_ge(w_ready, g + 1)
                for j in range(TOPK):
                    act.wait_ge(v_free, g * TOPK + j + 1)
                    eye = ident if t < SAMP else ident4
                    nc.scalar.activation(diag[j % VR][:, 0:n], eye[:, 0:n], ACT.Copy,
                                         scale=wts[:, j:j + 1]).then_inc(diag_ready, 1)
                    if g_is(g, 0) and j in (2, 3):
                        copy_head(j)
                    if g_is(g, 1) and j % 2 == 1:
                        copy_xnT(2 + j // 2)
                    for a, (tn, _, k) in zip(beside(g), nxt):
                        if j == a + 4:
                            copy_q(tn, k)
                        if j == a + 8:
                            copy_qT(tn, k)
                        if j == a + 10:
                            copy_s(tn, k)

            def copy_head(k):
                copy_q(0, k)
                copy_qT(0, k)
                copy_s(0, k)

            square_x2(0)
            copy_xnT(0)
            copy_xnT(1)
            copy_head(0)
            copy_head(1)
            for t in range(1, NT - 1):
                square_x2(t)
            for t in range(NT):
                n = TILES[t][1]
                loop, rest = steps_of(t)
                if loop:
                    with act.Fori(0, loop) as i:
                        step(t, i + FIRST[t], [(t + 1, i + 2, i + FIRST[t] + AHEAD + 1)])
                for g in rest:
                    for heads in gates_in(g):
                        exp_tops(*heads)
                    step(t, g, scored_in(g))
                act.wait_ge(v_free, VR + (FIRST[t] + STEPS[t]) * TOPK)
                copy(x[0:n, t, :], acc[0:n].rearrange("p a b -> p (a b)")).then_inc(acc_read, 1)
                act.wait_ge(acc_read, t + 1)
                nc.scalar.activation(xn[0:n, t, :], x[0:n, t, :], ACT.Square,
                                     accum_out=ssq[0:n, t:t + 1]).then_inc(summed, 1)
                root(t, summed, 2 * NT + t, y_squared)

        @block.vector
        def _(dve):
            made_ops = [0]
            vec = nc.vector

            def then(ins):
                made_ops[0] += 1
                ins.then_inc(dv, 1)
                dve.wait_ge(dv, made_ops[0])

            rms, rstd = small[:, 8:16], small[:, 16:24]

            def scaled_norm(t, out, src):
                n = TILES[t][1]
                then(vec.reciprocal(rstd[0:n, t:t + 1], rms[0:n, t:t + 1]))
                return vec.scalar_tensor_tensor(out=out, in0=src, scalar=rstd[0:n, t:t + 1], in1=gain[0:n, :],
                                                op0=ALU.mult, op1=ALU.mult)

            vec.memset(eps[:], EPS).then_inc(eps_set, 1)
            dve.wait_ge(gain_in, 16)
            for t, (a, n) in enumerate(TILES):
                dve.wait_ge(squared, t + 1)
                scaled_norm(t, h_stage[t % 2][0:n, :], x[0:n, t, :]).then_inc(h_ready, 1)

            dve.wait_ge(consts_in, 16 * N_CONST)
            w3 = w_s[:].rearrange("p (g i) -> p g i", g=GA)
            vec.tensor_tensor(w3, w3, tril[:].unsqueeze(1).to_broadcast([P, GA, P]), ALU.mult)
            vec.tensor_tensor(
                w_sb[0:NSAMP, :].rearrange("p (g b i) -> p g b i", g=GA, b=NB),
                blockm[0:NSAMP, :].rearrange("p (o b i) -> p o b i", o=1, b=NB).to_broadcast([NSAMP, GA, NB, NS]),
                w_s32[0:NSAMP, :].rearrange("p (g o i) -> p g o i", g=GA, o=1).to_broadcast([NSAMP, GA, NB, NS]),
                ALU.mult).then_inc(ws_ready, 1)

            def split_uv(t, u):
                n = TILES[t][1]
                ps = half(u % 3)
                st = lnst[0:n, 8 * t:8 * t + 8]
                dve.wait_ge(proj_done, u + 1)
                vec.tensor_copy(u_tok[0:n, t, :], ps[0:n, 0:DA])
                then(vec.bn_stats(st[:, 0:6], ps[0:n, DA:2 * DA]))
                vec.bn_aggr(st[:, 6:8], st[:, 0:6]).then_inc(ln_stats, 1)
                dve.wait_ge(ln_root, t + 1)
                then(vec.reciprocal(st[:, 7:8], st[:, 5:6]))
                v = vn[0:n, t, :]
                ins = vec.tensor_scalar(v, ps[0:n, DA:2 * DA], st[:, 6:7], st[:, 7:8], ALU.subtract, ALU.mult)
                ins.then_inc(uv_read, 1)
                dve.wait_ge(uv_read, t + 1)
                then(vec.tensor_tensor(v, v, lngb[0:n, 0, :], ALU.mult))
                then(vec.tensor_tensor(v, v, lngb[0:n, 1, :], ALU.add))

            def rotate(i, u):
                c, t = QK[i]
                n = TILES[t][1]
                nh = HALF // HD
                dve.wait_ge(qkv_read, u + 1 - NT)
                src = q_stage[i % 3] if CHUNKS[c][0] == "q" else k_stage[i - 2 * NT]
                xr = src[0:n, :].rearrange("p (h d) -> p h d", d=HD)
                ab = rope_ab[0:n, (i % 2) * 192:(i % 2) * 192 + 192].rearrange("p (a h d) -> p a h d", a=2, h=nh)
                cs = rope[0:n, 32 * t:32 * t + 32].rearrange("p (a o d) -> p a o d", a=4, o=1)
                vec.tensor_tensor(ab[:, 0], xr[:, :, 0:16],
                                  rope[0:n, 32 * t:32 * t + 16].unsqueeze(1).to_broadcast([n, nh, 16]), ALU.mult)
                vec.tensor_tensor(ab[:, 1, :, 0:8], xr[:, :, 8:16], cs[:, 2].to_broadcast([n, nh, 8]), ALU.mult)
                then(vec.tensor_tensor(ab[:, 1, :, 8:16], xr[:, :, 0:8], cs[:, 3].to_broadcast([n, nh, 8]), ALU.mult))
                vec.tensor_tensor(xr[:, :, 0:16], ab[:, 0], ab[:, 1], ALU.add).then_inc(roped, 1)

            for u, (c, t) in enumerate(UNITS):
                if CHUNKS[c][0] == "uv":
                    split_uv(t, u)
                elif (c, t) in qk_at:
                    rotate(qk_at[c, t], u)

            for t, (a, n) in enumerate(TILES):
                dve.wait_ge(mixed_done, t + 1)
                b0 = 0 if t < SAMP else GA
                ps = half(4 + t % 2)[0:n, 0:DA].rearrange("p (g d) -> p g d", g=GA)
                then(vec.tensor_tensor(ps, ps, bs[0:n, b0:b0 + GA].unsqueeze(2).to_broadcast([n, GA, HD]), ALU.add))
                u3 = u_tok[0:n, t, :]
                vec.tensor_tensor(u3, u3, half(4 + t % 2)[0:n, 0:DA], ALU.mult).then_inc(gated, 1)

            dve.wait_ge(kv_out, 16 * (3 * NT + 1))
            dve.wait_ge(qkT_ready, len(QK))

            def mask_max(u):
                unit = ATT[u]
                r, n = span(unit)
                st = att[:, 4 * (u % SR):4 * (u % SR) + 4]
                dve.wait_ge(scored, u + 1)
                if u >= SR:
                    dve.wait_ge(p_turned, u - SR + 1)

                def negated(out, scores, counts, least):
                    return vec.tensor_tensor_reduce(out=out, in0=scores, in1=counts, scale=-1.0, scalar=3e38,
                                                    op0=ALU.add, op1=ALU.min, accum_out=least)

                if unit[0] != "s":
                    negated(score[u % SR][:, 0:n], wide(u % 2, n), logc[:, 512 - n:512], st[:, 0:1]).then_inc(masked, 1)
                else:
                    b = unit[1]
                    negated(score[u % SR][0:r, 0:CK], wide(u % 2, CK)[0:r], smask[0:r, :], st[0:r, 1:2])
                    then(negated(score[u % SR][0:r, CK:n], wide(u % 2, n)[0:r, CK:n], snew[0:r, b, :], st[0:r, 3:4]))
                    vec.tensor_tensor(st[0:r, 0:1], st[0:r, 1:2], st[0:r, 3:4], ALU.min).then_inc(masked, 1)

            def normalise(u):
                r, n = span(ATT[u])
                st = att[:, 4 * (u % SR):4 * (u % SR) + 4]
                dve.wait_ge(exped, u + 1)
                then(vec.reciprocal(st[0:r, 3:4], st[0:r, 2:3]))
                vec.tensor_scalar(score[u % SR][0:r, 0:n], score[u % SR][0:r, 0:n], st[0:r, 3:4], None,
                                  ALU.mult).then_inc(normed, 1)

            def store_heads(u):
                unit = ATT[u]
                dve.wait_ge(pv_done, u + 1)
                out = half(6 + u % 2)
                if unit[0] != "s":
                    h, t = unit
                    r0 = HD * (h % 2)
                    vec.tensor_copy(featT[r0:r0 + HD, 2 + h // 2, t * P:(t + 1) * P],
                                    out[r0:r0 + HD, 0:P]).then_inc(att_ready, 1)
                else:
                    vec.tensor_copy(o_stage[0:OROWS, :], out[0:OROWS, 0:HALF]).then_inc(o_copied, 1)

            def store_sample(u):
                b = ATT[u][1]
                dve.wait_ge(o_turned, b + 1)
                w = OROWS + 2 * NS
                for f in range(2):
                    for s in range(2):
                        a = f * OTHERS + s * NS
                        src = half(6 + u % 2)[HD * s:HD * s + HD, a:a + 3 * w].rearrange("p (r w) -> p r w", w=w)
                        ins = vec.tensor_copy(featT[HD * s:HD * s + HD, 2 + 3 * f:5 + 3 * f,
                                                    SEQ + NS * b:SEQ + NS * b + NS], src[:, :, 0:NS])
                ins.then_inc(att_ready, 1)

            for u in range(len(ATT) + 5):
                if u < len(ATT):
                    mask_max(u)
                if 1 <= u <= len(ATT):
                    normalise(u - 1)
                if u >= 5 and ATT[u - 5][0] == "s":
                    store_sample(u - 5)
                if 4 <= u < len(ATT) + 4:
                    store_heads(u - 4)

            dve.wait_ge(gain_in, 32)

            def norm_x2(t):
                n = TILES[t][1]
                dve.wait_ge(squared2, t + 1)
                scaled_norm(t, xn[0:n, t, :], x[0:n, t, :]).then_inc(xn_ready, 1)

            def add_x(t, c):
                n = TILES[t][1]
                if c == 0:
                    dve.wait_ge(x_in[t], 32)
                dve.wait_ge(out_done, 2 * t + c + 1)
                xh = x[0:n, t, c * 512:(c + 1) * 512]
                vec.tensor_tensor(xh, xh, half(c)[0:n, :], ALU.add).then_inc(x2_ready, 1)

            def route(t, h, k, link):
                n = TILES[t][1]
                sc = [s_cur[s_buf(k)][0:n, c, :] for c in range(2)]
                sl = [s_left[0:n, c, :] for c in range(2)]
                wait_apart(dve, s_ready, k + 1)
                for c in range(2):
                    ins = vec.max(val[c][0:n, 0:8], sc[c])
                link(ins)
                for c in range(2):
                    vec.max_index(idx[c][0:n, 0:8], val[c][0:n, 0:8], sc[c])
                    ins = vec.match_replace(sl[c], val[c][0:n, 0:8], sc[c], -3e38)
                link(ins)
                for c in range(2):
                    ins = vec.max(val[c][0:n, 8:16], sl[c])
                link(ins)
                vec.tensor_tensor(cand[0:n, :].rearrange("p (i j) -> p i j", i=TOPK),
                                  val[0][0:n, :].unsqueeze(2).to_broadcast([n, TOPK, TOPK]),
                                  val[1][0:n, :].unsqueeze(1).to_broadcast([n, TOPK, TOPK]), ALU.add)
                for c in range(2):
                    ins = vec.max_index(idx[c][0:n, 8:16], val[c][0:n, 8:16], sl[c])
                link(ins)
                vec.max(top[0:n, 0:8], cand[0:n, :])
                for c in range(2):
                    ins = vec.tensor_copy(idf[c][0:n, :], idx[c][0:n, :])
                link(ins)
                vec.max_index(pos[0:n, 0:8], top[0:n, 0:8], cand[0:n, :])
                ins = vec.match_replace(cand_left[0:n, :], top[0:n, 0:8], cand[0:n, :], -3e38)
                link(ins)
                ins = vec.max(top[0:n, 8:16], cand_left[0:n, :])
                link(ins)
                vec.max_index(pos[0:n, 8:16], top[0:n, 8:16], cand_left[0:n, :])
                ins = vec.tensor_scalar(tops[0:n, bass.ds(h, 1), :].rearrange("p o k -> p (o k)"), top[0:n, :], top[0:n, 0:1],
                                  None, ALU.subtract)
                link(ins)
                vec.tensor_scalar(digit[0][0:n, :], pos[0:n, :], 4, None, ALU.logical_shift_right)
                ins = vec.tensor_scalar(digit[1][0:n, :], pos[0:n, :], TOPK - 1, None, ALU.bitwise_and)
                link(ins)
                for c in range(2):
                    ins = vec.tensor_tensor(hot[c][0:n], digit[c][0:n, :].unsqueeze(2).to_broadcast([n, TOPK, TOPK]),
                                      iota[0:n, :].unsqueeze(1).to_broadcast([n, TOPK, TOPK]), ALU.is_equal)
                link(ins)
                for c in range(2):
                    ins = vec.tensor_tensor(hot[c][0:n], hot[c][0:n], idf[c][0:n, :].unsqueeze(1).to_broadcast([n, TOPK, TOPK]),
                                      ALU.mult)
                link(ins)
                for c in range(2):
                    ins = vec.tensor_reduce(pick[c][0:n, :], hot[c][0:n], AX.X, ALU.add)
                link(ins)
                ins = vec.tensor_scalar(eidf[0:n, :], pick[0][0:n, :], float(NKEYS), None, ALU.mult)
                link(ins)
                dst = (eid[0:n, bass.ds(k * TOPK, TOPK)] if t < SAMP
                       else eid_samp[0:n, bass.ds(h * TOPK, TOPK)])
                vec.tensor_tensor(dst, eidf[0:n, :], pick[1][0:n, :], ALU.add).then_inc(
                    eid_ready if t < SAMP else eid_samp_ready, 1)

            def linker(start):
                done = [0]

                def link(ins):
                    done[0] += 1
                    ins.then_inc(route_link, 1)
                    wait_apart(dve, route_link, start + done[0])
                return link

            def finish_gates(t, lo, hi, n_exped):
                n = TILES[t][1]
                dve.wait_ge(tops_exped, n_exped)
                a, b = FIRST[t] + lo, FIRST[t] + hi
                g3 = (gate[0:n, a * TOPK:b * TOPK] if t < SAMP
                      else gate_samp[0:n, :]).rearrange("p (h k) -> p h k", h=hi - lo)
                then(vec.tensor_reduce(den8[0:n, lo:hi], tops[0:n, lo:hi], AX.X, ALU.add))
                then(vec.reciprocal(rden8[0:n, lo:hi], den8[0:n, lo:hi]))
                then(vec.tensor_tensor(g3, tops[0:n, lo:hi],
                                       rden8[0:n, lo:hi].unsqueeze(2).to_broadcast([n, hi - lo, TOPK]), ALU.mult))
                if t == SAMP:
                    to_groups(gate, gate_samp).then_inc(samp_gates, 1)
                    dve.wait_ge(samp_gates, 1)

            def to_groups(dst, src):
                a, m = FIRST[SAMP] * TOPK, SLOTS // GROUPS
                for g in range(GROUPS):
                    ins = vec.tensor_copy(dst[g * NSAMP:(g + 1) * NSAMP, a:a + m], src[0:NSAMP, g * m:(g + 1) * m])
                return ins

            def finish_y(t):
                n = TILES[t][1]
                s = rstd[0:n, t:t + 1]
                dve.wait_ge(y_squared, t + 1)
                then(vec.reciprocal(s, rms[0:n, t:t + 1]))
                vec.scalar_tensor_tensor(out=x[0:n, t, :], in0=x[0:n, t, :], scalar=s, in1=gain[0:n, :],
                                         op0=ALU.mult, op1=ALU.mult).then_inc(y_ready, 1)

            def set_x(t):
                if t < SAMP:
                    ins = vec.tensor_copy(x_cur, xn[:, t, :])
                else:
                    for g in range(GROUPS):
                        ins = vec.tensor_copy(x_cur[g * NSAMP:(g + 1) * NSAMP, :], xn[0:NSAMP, t, :])
                return ins

            def dots(g, lo, hi):
                for j in range(lo, hi):
                    s = j % UR
                    dve.wait_ge(u_landed[s], (g * (TOPK // UR) + j // UR + 1) * 16)
                    vec.tensor_tensor_reduce(out=u_ring[s], in0=u_ring[s], in1=x_cur, scale=1.0, scalar=0.0,
                                             op0=ALU.mult, op1=ALU.add, accum_out=hid[:, j:j + 1]).then_inc(u_free, 1)

            def weights(g):
                dve.wait_ge(gelu_done, g + 1)
                vec.tensor_tensor(wts[:], gelu[:], gate[:, bass.ds(g * TOPK, TOPK)], ALU.mult).then_inc(w_ready, 1)

            def step(g, gates, heads):
                dots(g, 0, TOPK)
                weights(g)
                for made in gates:
                    finish_gates(*made, n_gates[g])
                for tn, h, k in heads:
                    route(tn, h, k, linker(k * LINKS))

            n_gates = {g: sum(len(gates_in(i)) for i in range(g + 1)) for g in range(NSTEP)}
            add_x(0, 0)
            add_x(0, 1)
            norm_x2(0)
            dve.wait_ge(xn_ready, 1)
            set_x(0).then_inc(u_free, UR)
            dve.sem_inc(v_free, VR)
            add_x(1, 0)
            route(0, 0, 0, linker(0))
            add_x(1, 1)
            route(0, 1, 1, linker(LINKS))
            for i in range(4):
                add_x(2 + i // 2, i % 2)
                if i % 2 == 0:
                    norm_x2(1 + i // 2)
                dots(0, 4 * i, 4 * i + 4)
            finish_gates(*gates_in(0)[0], 1)
            weights(0)
            add_x(SAMP, 0)
            norm_x2(SAMP - 1)
            add_x(SAMP, 1)
            norm_x2(SAMP)
            for k in routed_in(0):
                route(0, k, k, linker(k * LINKS))
            for t in range(NT):
                loop, rest = steps_of(t)
                if loop:
                    with dve.Fori(0, loop) as i:
                        step(i + FIRST[t], [], [(t + 1, i + 1, i + FIRST[t] + AHEAD)])
                for g in rest:
                    if g == FIRST[SAMP] - 1:
                        dve.wait_ge(eid_samp_ready, HEADS)
                        to_groups(eid, eid_samp).then_inc(eid_ready, STEPS[SAMP])
                    if g > 0:
                        step(g, gates_in(g), [(k // HEADS, k % HEADS, k) for k in routed_in(g)])
                if t < SAMP:
                    then(set_x(t + 1))
                if t == 1:
                    dve.wait_ge(gain_in, 48)
                if t >= 1:
                    finish_y(t - 1)
            finish_y(SAMP)

        @block.gpsimd
        def _(pool):
            nc.gpsimd.dma_start(lngb, ln_gb.rearrange("(o a) d -> o a d", o=1).broadcast_to([P, 2, DA])).then_inc(consts_in, 16)
            for t, (a, n) in enumerate(TILES):
                nc.gpsimd.dma_start(rope[0:n, 32 * t:32 * t + 32], rope_c[a:a + n, :]).then_inc(consts_in, 16)
            nc.gpsimd.dma_start(w_s[:].rearrange("p (g i) -> p g i", g=GA), w_sT.rearrange("g j i -> j g i")).then_inc(consts_in, 16)
            for b in range(NB):
                nc.gpsimd.dma_start(w_s32[b * NS:(b + 1) * NS, :].rearrange("p (g i) -> p g i", g=GA),
                             w_sT[:, 0:NS, 0:NS].rearrange("g j i -> j g i")).then_inc(consts_in, 16)
                nc.gpsimd.dma_start(bs[b * NS:(b + 1) * NS, GA:2 * GA], b_sT[0:NS, :]).then_inc(consts_in, 16)
            nc.gpsimd.dma_start(bs[:, 0:GA], b_sT).then_inc(consts_in, 16)
            nc.gpsimd.dma_start(tril[:], tril_c).then_inc(consts_in, 16)
            nc.gpsimd.dma_start(blockm[0:NSAMP, :], blockm_c).then_inc(consts_in, 16)
            nc.gpsimd.dma_start(iota[:], iota_c).then_inc(consts_in, 16)
            nc.gpsimd.dma_start(logc, logc_c).then_inc(consts_in, 16)
            nc.gpsimd.dma_start(smask[0:SROWS, :], smask_c).then_inc(consts_in, 16)
            nc.gpsimd.dma_start(snew[0:SROWS], snew_c).then_inc(consts_in, 16)
            for g in range(GROUPS):
                nc.gpsimd.dma_start(ident4[g * NSAMP:(g + 1) * NSAMP, :], ident_c[0:NSAMP, 0:NSAMP]).then_inc(consts_in, 16)
            pool.wait_ge(kv_out, 16 * (3 * NT + 1))
            pool.wait_ge(qkT_ready, len(QK))
            for s in range(2):
                nc.gpsimd.memset(q_blk[s], 0.0).then_inc(qz, 1)
            pool.wait_ge(qz, 2)
            for b in range(NB):
                if b >= 2:
                    pool.wait_ge(scored, samp_at[b - 2] + 1)
                for s in range(2):
                    dst = blocks_of(q_blk[b % 2], HD * s, NS * s)
                    ins = nc.gpsimd.tensor_copy(dst, qT[HD * s:HD * s + HD, :, SEQ + NS * b:SEQ + NS * b + NS])
                ins.then_inc(qb_ready, 1)
                if b >= 2:
                    pool.wait_ge(pv_done, samp_at[b - 2] + 1)
                else:
                    pool.wait_ge(proj_done, len(UNITS))
                nc.gpsimd.dma_start(vc[b % 2], v_cache[b][0:CK, :].rearrange("(c p) n -> p c n", p=P)).then_inc(
                    vc_in[b % 2], 16)

            def gather(ring, indices, s, table, column, landed, n_staged):
                nc.gpsimd.tensor_copy(indices[:, s:s + 1], eid[:, bass.ds(column, 1)]).then_inc(staged, 1)
                wait_apart(pool, staged, n_staged)
                nc.gpsimd.indirect_dma_start(
                    out=ring[s], out_offset=None, in_=table,
                    in_offset=bass.IndirectOffsetOnAxis(ap=indices[:, s:s + 1], axis=0)).then_inc(landed[s], 16)

            pool.wait_ge(eid_ready, 1)
            for j in range(TOPK):
                pool.wait_ge(u_free, j + 1)
                gather(u_ring, u_idx, j % UR, u_tab, j, u_landed, j + 1)

            def step(g, more):
                if more:
                    wait_apart(pool, eid_ready, g + 2)
                for j in range(TOPK):
                    before = (g * 2 + 1) * TOPK + (2 * j if more else j)
                    if more:
                        wait_apart(pool, u_free, (g + 1) * TOPK + j + 1)
                        gather(u_ring, u_idx, j % UR, u_tab, (g + 1) * TOPK + j, u_landed, before + 1)
                    wait_apart(pool, v_free, g * TOPK + j + 1)
                    gather(v_ring, v_idx, j % VR, v_tab, g * TOPK + j, v_landed, before + (2 if more else 1))

            with pool.Fori(0, NSTEP - 1) as g:
                step(g, True)
            step(NSTEP - 1, False)


def counts_log(dist, reach):
    c = sum(((dist >= 0) & (dist <= w // d * d) & (dist % d == 0) & reach).astype(np.int64) for w, d in BRANCHES)
    return np.where(c > 0, np.log(np.maximum(c, 1)), NEG).astype(np.float32)


def shape_tables():
    r = np.arange(P)
    ident = np.eye(P, dtype=np.float32)
    logc = counts_log(r[:, None] - np.arange(512)[None, :] + 384, True)
    m = np.arange(STRIDED)
    first = 16 * (m // NS) + m % NS
    near = np.arange(PAST - NEAR, PAST)
    rest = np.setdiff1d(np.arange(PAST), np.concatenate([first, near]))
    order = np.concatenate([first, near, rest])
    q = np.tile(np.arange(NS), NH)
    smask = counts_log(PAST + q[:, None] - order[None, :CK], True)
    new_b, new_j = np.arange(NEWK) // NS, np.arange(NEWK) % NS
    snew = np.stack([counts_log(q[:, None] - new_j[None, :], new_b[None, :] == b) for b in range(NB)], axis=1)
    pos = np.concatenate([np.arange(SEQ), PAST + np.tile(np.arange(NS), NB)]).astype(np.float32)
    rot = HD // 4
    inv = np.float32(500000.0) ** (-np.arange(0, rot, 2, dtype=np.float32) / np.float32(rot))
    ang = pos[:, None] * inv[None, :].astype(np.float32)
    c, s = np.cos(ang), np.sin(ang)
    rope = np.concatenate([c, c, -s, s], axis=1).astype(np.float32)
    iota = np.tile(np.arange(TOPK, dtype=np.float32), (P, 1))
    tril = (r[:, None] <= r[None, :]).astype(np.float32)
    b, i = np.arange(NSAMP) // NS, np.arange(NSAMP) % NS
    blockm = ((b[:, None] == b[None, :]) & (i[:, None] <= i[None, :])).astype(np.float32)
    return order, dict(ident_c=ident, logc_c=logc, smask_c=smask, snew_c=snew, rope_c=rope, iota_c=iota,
                       tril_c=tril, blockm_c=blockm)


def kernel(x_prompt, x_sample, cache_k_win, cache_v_win, attn_norm, w_in, ln_v_g, ln_v_b, w_s, b_s, w_out,
           ffn_norm, peer_w_q, peer_sub_keys, peer_u, peer_v, final_norm):
    import concourse.bacc as bacc
    from concourse.bass_utils import run_bass_kernel_spmd

    f = np.asarray
    order, tables = shape_tables()
    arrays = dict(
        x_p=f(x_prompt)[0], x_s=f(x_sample).reshape(NSAMP, D),
        k_cache=f(cache_k_win)[0].reshape(NB, PAST, DB)[:, order].transpose(0, 2, 1),
        v_cache=f(cache_v_win)[0].reshape(NB, PAST, DB)[:, order],
        gains=np.stack([f(attn_norm)[0], f(ffn_norm)[0], f(final_norm)]),
        w_in=f(w_in)[0], ln_gb=np.stack([f(ln_v_g)[0], f(ln_v_b)[0]]),
        w_sT=f(w_s)[0].transpose(0, 2, 1), b_sT=f(b_s)[0].T, w_out=f(w_out)[0], w_q=f(peer_w_q)[0],
        keysT=f(peer_sub_keys)[0].reshape(2 * HEADS * NKEYS, P).T, u_tab=f(peer_u)[0], v_tab=f(peer_v)[0],
        **tables)
    outs = dict(y_p=(SEQ, D), y_s=(NSAMP, D), k_p=(SEQ, DB), v_p=(SEQ, DB), k_s=(NSAMP, DB), v_s=(NSAMP, DB),
                gv_s=(NSAMP, DA))
    nc = bacc.Bacc("TRN2", target_bir_lowering=False, num_devices=1)
    aps, feeds = {}, {}
    for name, a in arrays.items():
        a = np.ascontiguousarray(a)
        feeds["in_" + name] = a
        aps[name] = nc.dram_tensor("in_" + name, a.shape, mybir.dt.from_np(a.dtype), kind="ExternalInput").ap()
    for name, shape in outs.items():
        aps[name] = nc.dram_tensor("out_" + name, shape, F32, kind="ExternalOutput").ap()
    build(nc, **aps)
    got = run_bass_kernel_spmd(nc, [feeds], core_ids=[0]).results[0]
    y_p, y_s, k_p, v_p, k_s, v_s, gv_s = (got["out_" + name] for name in outs)
    return (y_p.reshape(1, SEQ, D), y_s.reshape(NB, NS, D),
            k_p.reshape(1, 1, SEQ, NH, HD), v_p.reshape(1, 1, SEQ, NH, HD),
            k_s.reshape(1, NB, NS, NH, HD), v_s.reshape(1, NB, NS, NH, HD), gv_s.reshape(1, NB, NS, DA))
```

```python
import math
from contextlib import ExitStack

import numpy as np

import concourse.bass as bass
from concourse import mybir
from concourse.alu_op_type import AluOpType as ALU

ACT = mybir.ActivationFunctionType
AX = mybir.AxisListType
F32 = mybir.dt.float32
U32 = mybir.dt.uint32

P = 128
D = 1024
KD = D // P
SEQ = 512
NB, NS = 8, 4
NSAMP = NB * NS
PAST = 1024
DA, DB, NH, HD = 256, 768, 12, 64
GA = 4
PAIRS = NH // 2
TOK = SEQ + NSAMP
TILES = [(t * P, P) for t in range(SEQ // P)] + [(SEQ, NSAMP)]
NT = len(TILES)
SAMP = NT - 1
HALF = DB // 2
CHUNKS = [("uv", 0, 2 * DA)] + [(n, 2 * DA + i * DB + j * HALF, HALF)
                                for i, n in enumerate("qkv") for j in range(2)]
BRANCHES = ((128, 1), (512, 4), (2048, 16))
NEG = -1e30
EPS = 1e-6
STRIDED = 128
NEAR = 512
CK = STRIDED + NEAR
NEWK = NSAMP
SROWS = NH * NS
SCOLS = CK + NEWK
CG, NCG = 32, 3
OUT_COLS = ((0, 192), (192, 384), (384, 512))
GROWS = SROWS // NCG

HEADS = 8
NKEYS = 128
TOPK = 16
SLOTS = HEADS * TOPK
UR, VR = 8, 4
GROUPS = P // NSAMP
LINKS = 13
STEPS = [HEADS] * (NT - 1) + [HEADS // GROUPS]
FIRST = [sum(STEPS[:t]) for t in range(NT)]
NSTEP = sum(STEPS)


def build(nc, x_p, x_s, k_cache, v_cache, gains, w_in, ln_gb, w_sT, b_sT, w_out, w_q, keysT, u_tab, v_tab,
          ident_c, logc_c, smask_c, snew_c, rope_c, iota_c, tril_c, blockm_c,
          y_p, y_s, k_p, v_p, k_s, v_s, gv_s):
    ctx = ExitStack()
    with ctx:
        def sb(name, n, dt=F32):
            return ctx.enter_context(nc.sbuf_tensor(name, [P, n], dt))

        def sem(name):
            return ctx.enter_context(nc.semaphore(name))

        area_w = sb("area_w", 16384)
        area_r = sb("area_r", 14720)
        area_t = sb("area_t", KD * TOK)
        area_x = sb("area_x", NT * D)
        area_v = sb("area_v", 6400)
        area_c = sb("area_c", 2176)

        def cut(area, a, *dims):
            n = math.prod(dims)
            v = area[:, a:a + n]
            if len(dims) == 2:
                v = v.rearrange("p (a b) -> p a b", a=dims[0])
            if len(dims) == 3:
                v = v.rearrange("p (a b c) -> p a b c", a=dims[0], b=dims[1])
            return v

        W_SLOTS = 4
        w_ring = [cut(area_w, s * KD * 512, KD, 512) for s in range(W_SLOTS)]
        kc = [cut(area_w, (1 - s) * 2 * PAIRS * CK, PAIRS, CK) for s in range(2)]
        vc = [cut(area_w, ((1 - s) * 2 + 1) * PAIRS * CK, CK // P, DB) for s in range(2)]
        w_o = cut(area_w, KD * D, KD, D)
        WQ = KD * 2 * P
        wq = [cut(area_w, h * WQ, KD, 2 * P) for h in range(HEADS)]

        qT = cut(area_r, KD * D, PAIRS, TOK)
        kT = cut(area_r, KD * D + PAIRS * TOK, PAIRS, TOK)
        u_ring = [cut(area_r, s * D, D) for s in range(UR)]
        v_ring = [cut(area_r, (UR + s) * D, D) for s in range(VR)]
        keys = cut(area_r, (UR + VR) * D, 2 * HEADS * NKEYS)

        featT = cut(area_t, 0, KD, TOK)

        x = cut(area_x, 0, NT, D)
        SR = 4
        q_stage = [cut(area_x, s * HALF, HALF) for s in range(3)]
        k_stage = [cut(area_x, (3 + s) * HALF, HALF) for s in range(2 * NT)]
        score = [cut(area_x, s * SCOLS, SCOLS) for s in range(SR)]
        probT = [cut(area_x, SR * SCOLS + s * 512, 512) for s in range(2)]
        QB = PAIRS * CG
        q_blk = [cut(area_x, SR * SCOLS + 1024 + s * QB, QB) for s in range(2)]

        OROWS = (NCG - 1) * CG + GROWS
        o_stage = cut(area_x, SR * SCOLS + 1024 + 2 * QB, DB // NCG)

        h_stage = [cut(area_v, s * D, D) for s in range(2)]
        v_tok = cut(area_v, 0, NT, DB)
        u_tok = cut(area_v, NT * DB, NT, DA)
        vn = cut(area_v, NT * (DB + DA), NT, DA)
        xn = cut(area_v, 0, NT, D)

        logc = cut(area_c, 0, 512)
        smask = cut(area_c, 512, CK)
        snew = cut(area_c, 512 + CK, NB, NEWK)
        lngb = cut(area_c, 512 + CK + NB * NEWK, 2, DA)

        gain = sb("gain", D)
        ident = sb("ident", P)
        w_s = sb("w_s", GA * P)
        w_s32 = sb("w_s32", GA * NS)
        w_sb = sb("w_sb", GA * NSAMP)
        bs = sb("bs", 2 * GA)
        tril = sb("tril", P)
        blockm = sb("blockm", NSAMP)
        rope = sb("rope", NT * 32)
        rope_ab = sb("rope_ab", 4 * 96)
        iota = sb("iota", TOPK)
        small = sb("small", 24)
        eps = sb("eps", 1)
        lnst = sb("lnst", NT * 8)
        att = sb("att", SR * 4)

        eid = sb("eid", NSTEP * TOPK, U32)
        gate = sb("gate", NSTEP * TOPK)
        u_idx = sb("u_idx", UR, U32)
        v_idx = sb("v_idx", VR, U32)
        hid = sb("hid", TOPK)
        gelu = sb("gelu", TOPK)
        wts = sb("wts", TOPK)
        ident4 = sb("ident4", NSAMP)

        diag = [cut(area_c, s * P, P) for s in range(VR)]
        q_row = cut(area_c, 512, 2 * P)
        q_col = cut(area_c, 768, 2, P)
        s_cur = [cut(area_v, NT * D + a, 2, NKEYS) for a in (0, 1024)]
        s_left = cut(area_v, NT * D + 256, 2, NKEYS)
        cand = cut(area_c, 1024, TOPK * TOPK)
        cand_left = cut(area_c, 1280, TOPK * TOPK)
        hot = [cut(area_v, NT * D + 512 + c * 256, TOPK, TOPK) for c in range(2)]
        tops = cut(area_c, 1536, HEADS, TOPK)
        eid_samp = cut(area_c, 1664, SLOTS)
        gate_samp = cut(area_c, 1792, SLOTS)
        rt = cut(area_c, 1920, 9 * TOPK)
        rtu = sb("rtu", 5 * TOPK, U32)
        val = [rt[:, c * TOPK:(c + 1) * TOPK] for c in range(2)]
        idf = [rt[:, (2 + c) * TOPK:(3 + c) * TOPK] for c in range(2)]
        pick = [rt[:, (4 + c) * TOPK:(5 + c) * TOPK] for c in range(2)]
        top = rt[:, 6 * TOPK:7 * TOPK]
        den8 = rt[:, 7 * TOPK:7 * TOPK + 8]
        rden8 = rt[:, 7 * TOPK + 8:8 * TOPK]
        eidf = rt[:, 8 * TOPK:9 * TOPK]
        idx = [rtu[:, c * TOPK:(c + 1) * TOPK] for c in range(2)]
        pos = rtu[:, 2 * TOPK:3 * TOPK]
        digit = [rtu[:, (3 + c) * TOPK:(4 + c) * TOPK] for c in range(2)]

        bank = [ctx.enter_context(nc.psum_tensor(f"bank{i}", [P, 2, 512], F32)) for i in range(4)]

        def half(i):
            return bank[i // 2][:, i % 2, :]

        def wide(i, n):
            return bank[i].rearrange("p a b -> p (a b)")[:, 0:n]

        acc = bank[0]
        x_cur = wide(1, D)
        ps_q, ps_qT, ps_s = half(4), half(5), half(6)

        x_in = [sem(f"x_in{t}") for t in range(NT)]
        ident_in, consts_in, gain_in = sem("ident_in"), sem("consts_in"), sem("gain_in")
        w_in_sem = [sem(f"w_in{s}") for s in range(W_SLOTS)]
        w_out_in, keys_in = sem("w_out_in"), sem("keys_in")
        wq_in = [sem(f"wq_in{h}") for h in range(HEADS)]
        kc_in = [sem(f"kc_in{s}") for s in range(2)]
        vc_in = [sem(f"vc_in{s}") for s in range(2)]
        k_out, v_out, y_out = sem("k_out"), sem("v_out"), sem("y_out")
        dv = sem("dv")
        eps_set, summed, ln_stats, ln_root = sem("eps_set"), sem("summed"), sem("ln_stats"), sem("ln_root")
        squared, h_ready, h_turned, hT_ready = sem("squared"), sem("h_ready"), sem("h_turned"), sem("hT_ready")
        proj_done, uv_read, qkv_read = sem("proj_done"), sem("uv_read"), sem("qkv_read")
        roped, qk_turned, qkT_ready = sem("roped"), sem("qk_turned"), sem("qkT_ready")
        ws_ready, mixed_done, gated, g_turned, gT_ready = (sem("ws_ready"), sem("mixed_done"), sem("gated"),
                                                           sem("g_turned"), sem("gT_ready"))
        qb_ready, scored, masked, exped, normed = (sem("qb_ready"), sem("scored"), sem("masked"), sem("exped"),
                                                   sem("normed"))
        p_turned, pT_ready, pv_done, att_ready = sem("p_turned"), sem("pT_ready"), sem("pv_done"), sem("att_ready")
        o_copied, o_turned = sem("o_copied"), sem("o_turned")
        out_done, x2_ready, squared2, xn_ready = sem("out_done"), sem("x2_ready"), sem("squared2"), sem("xn_ready")
        xn_turned, xnT_ready = sem("xn_turned"), sem("xnT_ready")
        qz = sem("qz")
        q_done, q_copied, q_turned, qT_copied = sem("q_done"), sem("q_copied"), sem("q_turned"), sem("qT_copied")
        s_done, s_ready = sem("s_done"), sem("s_ready")
        tops_exped = sem("tops_exped")
        u_landed = [sem(f"u_landed{s}") for s in range(UR)]
        v_landed = [sem(f"v_landed{s}") for s in range(VR)]
        u_free, v_free = sem("u_free"), sem("v_free")
        staged = sem("staged")
        gelu_done, w_ready, diag_ready = sem("gelu_done"), sem("w_ready"), sem("diag_ready")
        passed = sem("passed")
        samp_gates = sem("samp_gates")
        eid_ready, eid_samp_ready = sem("eid_ready"), sem("eid_samp_ready")
        route_link = sem("route_link")
        acc_read, y_squared, y_ready = sem("acc_read"), sem("y_squared"), sem("y_ready")

        block = ctx.enter_context(nc.Block())

        N_CONST = 1 + NT + 1 + 2 * NB + 7 + GROUPS
        UNITS = [(c, t) for c in range(len(CHUNKS)) for t in range(NT)]
        QK = [(c, t) for c, t in UNITS if CHUNKS[c][0] in "qk"]
        qk_at = {u: i for i, u in enumerate(QK)}
        N_QKV = len(UNITS) - NT
        ATT, GROUP = [], []
        for i in range(PAIRS * (NT - 1)):
            pr, t = i // (NT - 1), i % (NT - 1)
            GROUP.append([len(ATT), len(ATT) + 1])
            ATT += [(2 * pr, t), (2 * pr + 1, t)]
            if i % 3 == 2:
                GROUP.append([len(ATT)])
                ATT.append(("s", i // 3))
        NG = len(GROUP)

        def group(i):
            return GROUP[i] if 0 <= i < NG else []

        samp_at = {b: ATT.index(("s", b)) for b in range(NB)}
        NOUT = 2 * 2 * NT
        GMLP_AT = [3 * NT + 2 * t for t in range(NT)]

        AHEAD = HEADS + 1
        N_ROUTED = HEADS * NT

        def routed_in(g):
            ks = (2 * g + 2, 2 * g + 3) if g < HEADS - 1 else (g + AHEAD,)
            return [k for k in ks if k < N_ROUTED]

        def scored_in(g):
            return [(k // HEADS, k % HEADS, k) for k in routed_in(g + 1)]

        def steps_of(t):
            loop = STEPS[t] - 2 if t > 0 else 0
            return loop, range(FIRST[t] + loop, FIRST[t] + STEPS[t])

        def gates_in(g):
            if g < HEADS // 2:
                return [(0, 2 * g, 2 * g + 2)]
            if g % HEADS == HEADS - 1 and g // HEADS < SAMP:
                return [(g // HEADS + 1, 0, HEADS)]
            return []

        def s_buf(k):
            return k % 2 if isinstance(k, int) and k < 2 * HEADS else 0

        def g_is(g, number):
            return isinstance(g, int) and g == number

        def beside(g):
            return (3, 5) if g_is(g, 0) else (0, 2)

        def grouped(c, t):
            return t == SAMP

        def span(u):
            return (P, (u[1] + 1) * P) if u[0] != "s" else (NCG * CG, SCOLS)

        def wait_apart(engine, what, value):
            engine.wait_ge(what, value)
            engine.sem_inc(passed, 1)

        def peer_x(t):
            return NSAMP if t == SAMP else P

        @block.sync
        def _(sp):
            for t, (a, n) in enumerate(TILES):
                src = x_p[a:a + n, :] if t < SAMP else x_s
                sp.dma_start(x[0:n, t, :], src).then_inc(x_in[t], 16)
                if t == 0:
                    sp.dma_start(gain[:], gains[0:1, :].broadcast_to([P, D])).then_inc(gain_in, 16)
                    sp.dma_start(ident[:], ident_c).then_inc(ident_in, 16)

            def load_w(c):
                s = c % W_SLOTS
                _, a, n = CHUNKS[c]
                sp.dma_start(w_ring[s][:, :, 0:n],
                             w_in[:, a:a + n].rearrange("(k p) n -> p k n", p=P)).then_inc(w_in_sem[s], 16)

            load_w(0)
            load_w(1)
            load_w(2)
            load_w(3)
            for c in range(W_SLOTS, len(CHUNKS)):
                sp.wait_ge(proj_done, NT * (c - W_SLOTS + 1))
                load_w(c)
            sp.wait_ge(h_ready, NT)
            sp.dma_start(gain[:], gains[1:2, :].broadcast_to([P, D])).then_inc(gain_in, 16)
            for c, t in QK:
                if CHUNKS[c][0] == "k":
                    i, (a, n) = qk_at[c, t], TILES[t]
                    sp.wait_ge(roped, i + 1)
                    dst, a = (k_p, a) if t < SAMP else (k_s, 0)
                    j = CHUNKS[c][1] - 2 * DA - DB
                    sp.dma_start(dst[a:a + n, j:j + HALF], k_stage[i - 2 * NT][0:n, :]).then_inc(k_out, 16)
            def load_keys(b):
                sp.dma_start(kc[b % 2], k_cache[b][:, 0:CK].rearrange("(r p) n -> p r n", p=P)).then_inc(kc_in[b % 2], 16)

            sp.wait_ge(proj_done, len(UNITS))
            load_keys(0)
            sp.wait_ge(qkv_read, N_QKV)
            for t, (a, n) in enumerate(TILES):
                dst, a = (v_p, a) if t < SAMP else (v_s, 0)
                sp.dma_start(dst[a:a + n, :], v_tok[0:n, t, :]).then_inc(v_out, 16)
            sp.dma_start(gv_s, vn[0:NSAMP, SAMP, :]).then_inc(v_out, 16)
            for b in range(1, NB):
                if b >= 2:
                    sp.wait_ge(scored, samp_at[b - 2] + 1)
                load_keys(b)
            sp.wait_ge(pv_done, samp_at[NB - 2] + 1)
            sp.dma_start(w_o, w_out.rearrange("(k p) n -> p k n", p=P)).then_inc(w_out_in, 16)
            sp.wait_ge(pv_done, len(ATT))
            sp.wait_ge(qb_ready, NB)
            sp.wait_ge(o_turned, NB)
            def load_x_again(t):
                a, n = TILES[t]
                src = x_p[a:a + n, :] if t < SAMP else x_s
                sp.dma_start(x[0:n, t, :], src).then_inc(x_in[t], 16)

            def load_wq(h):
                sp.dma_start(wq[h], w_q[:, 2 * P * h:2 * P * (h + 1)].rearrange("(k p) n -> p k n", p=P)).then_inc(
                    wq_in[h], 16)

            load_x_again(0)
            load_wq(0)
            load_x_again(1)
            load_wq(1)
            sp.dma_start(keys, keysT).then_inc(keys_in, 16)
            for t in range(2, NT):
                load_x_again(t)
            for h in range(2, HEADS // 2):
                load_wq(h)
            sp.wait_ge(out_done, 2 * NT)
            for h in range(HEADS // 2, HEADS):
                load_wq(h)
            sp.wait_ge(xn_ready, NT)
            sp.dma_start(gain[:], gains[2:3, :].broadcast_to([P, D])).then_inc(gain_in, 16)
            for t, (a, n) in enumerate(TILES):
                sp.wait_ge(y_ready, t + 1)
                dst = y_p[a:a + n, :] if t < SAMP else y_s
                sp.dma_start(dst, x[0:n, t, :]).then_inc(y_out, 16)
            sp.wait_ge(y_out, 16 * NT)
            sp.wait_ge(k_out, 16 * 2 * NT)
            sp.wait_ge(v_out, 16 * (NT + 1))

        @block.tensor
        def _(pe):
            pe.wait_ge(ident_in, 16)

            def turn(out, src, n):
                return pe.transpose(out, src, ident[0:n, 0:n])

            def turn_h(t):
                n = TILES[t][1]
                pe.wait_ge(h_ready, t + 1)
                if t >= 2:
                    pe.wait_ge(hT_ready, t - 1)
                dst = bank[2 + t % 2]
                for k in range(KD):
                    mm = turn(dst[:, k // 4, (k % 4) * P:(k % 4) * P + n], h_stage[t % 2][0:n, k * P:(k + 1) * P], n)
                mm.then_inc(h_turned, 1)

            def turn_qk(i):
                c, t = QK[i]
                n = TILES[t][1]
                pe.wait_ge(roped, i + 1)
                if i >= 2:
                    pe.wait_ge(qkT_ready, i - 1)
                else:
                    pe.wait_ge(hT_ready, NT)
                src = q_stage[i % 3] if CHUNKS[c][0] == "q" else k_stage[i - 2 * NT]
                for j in range(3):
                    mm = turn(half(4 + i % 2)[:, j * P:j * P + n], src[0:n, j * P:(j + 1) * P], n)
                mm.then_inc(qk_turned, 1)

            def gmlp(t):
                n = TILES[t][1]
                if t == 0:
                    pe.wait_ge(ws_ready, 1)
                if t >= 2:
                    pe.wait_ge(gated, t - 1)
                for g in range(GA):
                    lhs = w_s[:, g * P:(g + 1) * P] if t < SAMP else w_sb[0:n, g * NSAMP:(g + 1) * NSAMP]
                    mm = pe.matmul(half(6 + t % 2)[0:n, g * HD:(g + 1) * HD], lhs, vn[0:n, t, g * HD:(g + 1) * HD],
                                   start=True, stop=True)
                mm.then_inc(mixed_done, 1)

            for u, (c, t) in enumerate(UNITS):
                a, n = TILES[t]
                w = CHUNKS[c][2]
                if u == 0:
                    turn_h(0)
                if u + 1 < NT:
                    turn_h(u + 1)
                if t == 0:
                    pe.wait_ge(w_in_sem[c % W_SLOTS], 16 * (c // W_SLOTS + 1))
                if c == 0:
                    pe.wait_ge(hT_ready, t + 1)
                if 3 <= u < NT + 3:
                    pe.wait_ge(uv_read, u - 2)
                elif u >= NT + 3:
                    pe.wait_ge(qkv_read, u - 2 - NT)
                for k in range(KD):
                    if grouped(c, t):
                        m = DA if c == 0 else P
                        for g in range(w // m):
                            mm = pe.matmul(half(u % 3)[CG * g:CG * g + n, 0:m], featT[:, k, a:a + n],
                                           w_ring[c % W_SLOTS][:, k, g * m:(g + 1) * m], start=(k == 0), stop=(k == KD - 1))
                    else:
                        mm = pe.matmul(half(u % 3)[0:n, 0:w], featT[:, k, a:a + n], w_ring[c % W_SLOTS][:, k, 0:w],
                                       start=(k == 0), stop=(k == KD - 1))
                mm.then_inc(proj_done, 1)
                if u >= 2 and UNITS[u - 2] in qk_at:
                    turn_qk(qk_at[UNITS[u - 2]])
                if u in GMLP_AT:
                    gmlp(GMLP_AT.index(u))

            def turn_gated(t):
                n = TILES[t][1]
                pe.wait_ge(gated, NT)
                if t >= 2:
                    pe.wait_ge(gT_ready, t - 1)
                for k in range(2):
                    mm = turn(half(6 + t % 2)[:, k * P:k * P + n], u_tok[0:n, t, k * P:(k + 1) * P], n)
                mm.then_inc(g_turned, 1)

            for t in range(NT):
                turn_gated(t)
            pe.wait_ge(qkT_ready, len(QK))
            pe.wait_ge(gT_ready, NT)
            pe.wait_ge(qkv_read, N_QKV)

            def scores(u):
                unit = ATT[u]
                if u >= 2:
                    pe.wait_ge(masked, u - 1)
                if unit[0] != "s":
                    h, t = unit
                    r0, pr = HD * (h % 2), h // 2
                    n = (t + 1) * P
                    mm = pe.matmul(wide(u % 2, n), qT[r0:r0 + HD, pr, t * P:(t + 1) * P], kT[r0:r0 + HD, pr, 0:n],
                                   start=True, stop=True)
                else:
                    b = unit[1]
                    pe.wait_ge(qb_ready, b + 1)
                    pe.wait_ge(kc_in[b % 2], 16 * (b // 2 + 1))
                    for lo, hi, src in ((0, 512, kc[b % 2][:, :, 0:512]), (512, CK, kc[b % 2][:, :, 512:CK]),
                                        (CK, SCOLS, kT[:, :, SEQ:TOK])):
                        for i in range(2):
                            for g in range(NCG):
                                pr = 2 * g + i
                                mm = pe.matmul(wide(u % 2, D)[CG * g:CG * g + CG, lo:hi],
                                               q_blk[b % 2][:, pr * CG:(pr + 1) * CG],
                                               src[:, pr, :], start=(i == 0), stop=(i == 1))
                mm.then_inc(scored, 1)

            def turn_probs(u):
                r, n = span(ATT[u])
                pe.wait_ge(normed, u + 1)
                if u >= 2:
                    pe.wait_ge(pT_ready, u - 1)
                for j, a in enumerate(range(0, n, P)):
                    w = min(P, n - a)
                    if ATT[u][0] != "s":
                        mm = turn(half(4 + u % 2)[0:w, j * r:(j + 1) * r], score[u % SR][0:r, a:a + w], r)
                    else:
                        rows = ident[0:r, 0:r].rearrange("p (g w) -> p g w", w=CG)[:, :, 0:GROWS]
                        out = half(4 + u % 2)[0:w, j * SROWS:(j + 1) * SROWS].rearrange("p (g w) -> p g w", w=GROWS)
                        mm = pe.matmul(out, score[u % SR][0:r, a:a + w], rows, start=True, stop=True)
                mm.then_inc(p_turned, 1)

            def outputs(us):
                for u in us:
                    pe.wait_ge(pT_ready, u + 1)
                    if u >= 2:
                        pe.wait_ge(att_ready, u - 1)
                u, unit, out = us[0], ATT[us[0]], half(6 + us[0] % 2)
                if unit[0] != "s":
                    t = unit[1]
                    for j in range(t + 1):
                        for u in us:
                            h = ATT[u][0]
                            r0 = HD * (h % 2)
                            mm = pe.matmul(half(6 + u % 2)[r0:r0 + HD, 0:P], v_tok[:, j, h * HD:(h + 1) * HD],
                                           probT[u % 2][:, j * P:(j + 1) * P], start=(j == 0), stop=(j == t))
                            if j == t and u == us[0]:
                                mm.then_inc(pv_done, 1)
                else:
                    b = unit[1]
                    pe.wait_ge(vc_in[b % 2], 16 * (b // 2 + 1))
                    for j in range(CK // P + 1):
                        new = j == CK // P
                        nk = NEWK if new else P
                        v = v_tok[0:NEWK, SAMP] if new else vc[b % 2][:, j]
                        for g in range(NCG):
                            rows = CG if g < NCG - 1 else GROWS
                            a = j * SROWS + g * GROWS
                            mm = pe.matmul(out[CG * g:CG * g + rows, 0:DB // NCG], probT[u % 2][0:nk, a:a + rows],
                                           v[:, g * (DB // NCG):(g + 1) * (DB // NCG)], start=(j == 0), stop=new)
                mm.then_inc(pv_done, 1)

            def turn_outputs(u):
                pe.wait_ge(o_copied, ATT[u][1] + 1)
                for c in range(2):
                    mm = turn(half(6 + u % 2)[:, c * OROWS:(c + 1) * OROWS], o_stage[0:OROWS, c * P:(c + 1) * P], OROWS)
                mm.then_inc(o_turned, 1)

            for i in range(NG + 3):
                for u in group(i):
                    scores(u)
                for u in group(i - 3):
                    if ATT[u][0] == "s":
                        turn_outputs(u)
                for u in group(i - 1):
                    turn_probs(u)
                if group(i - 2):
                    outputs(group(i - 2))

            def project_out(t, c):
                a, n = TILES[t]
                v = 2 * t + c
                if v >= 2:
                    pe.wait_ge(x2_ready, v - 1)
                if t < SAMP:
                    for k in range(KD):
                        mm = pe.matmul(half(c)[0:n, :], featT[:, k, a:a + n], w_o[:, k, c * 512:(c + 1) * 512],
                                       start=(k == 0), stop=(k == KD - 1))
                else:
                    for k in range(KD):
                        for g, (lo, hi) in enumerate(OUT_COLS):
                            pe.matmul(half(c)[CG * g:CG * g + n, 0:hi - lo], featT[:, k, a:a + n],
                                      w_o[:, k, c * 512 + lo:c * 512 + hi], start=(k == 0), stop=False)
                    pe.wait_ge(x_in[t], 32)
                    for g, (lo, hi) in enumerate(OUT_COLS):
                        mm = pe.matmul(half(c)[CG * g:CG * g + n, 0:hi - lo], ident[0:n, 0:n],
                                       x[0:n, t, c * 512 + lo:c * 512 + hi], start=False, stop=True)
                mm.then_inc(out_done, 1)

            def turn_xn(v):
                t, n = v // 2, TILES[v // 2][1]
                pe.wait_ge(xn_ready, t + 1)
                if v >= 1:
                    pe.wait_ge(xnT_ready, v)
                for k in range(4):
                    f = (v % 2 * 4 + k) * P
                    mm = turn(half(7)[:, k * P:k * P + n], xn[0:n, t, f:f + P], n)
                mm.then_inc(xn_turned, 1)

            def queries(t, h, n_done):
                a, n = TILES[t]
                if not isinstance(n_done, int) or n_done:
                    pe.wait_ge(q_copied, n_done)
                for k in range(KD):
                    mm = pe.matmul(ps_q[0:n, 0:2 * P], featT[:, k, a:a + n], area_w[:, bass.ds(h * WQ + k * 2 * P, 2 * P)],
                                   start=(k == 0), stop=(k == KD - 1))
                mm.then_inc(q_done, 1)

            def turn_queries(t, n_done):
                n = TILES[t][1]
                wait_apart(pe, q_copied, n_done + 1)
                if not isinstance(n_done, int) or n_done:
                    wait_apart(pe, qT_copied, n_done)
                for c in range(2):
                    mm = turn(ps_qT[:, c * P:c * P + n], q_row[0:n, c * P:(c + 1) * P], n)
                mm.then_inc(q_turned, 1)

            def key_scores(t, h, n_done):
                n = TILES[t][1]
                pe.wait_ge(qT_copied, n_done + 1)
                if not isinstance(n_done, int) or n_done:
                    pe.wait_ge(s_ready, n_done)
                for c in range(2):
                    mm = pe.matmul(ps_s[0:n, c * NKEYS:(c + 1) * NKEYS], q_col[:, c, 0:n],
                                   keys[:, bass.ds((2 * h + c) * NKEYS, NKEYS)], start=True, stop=True)
                mm.then_inc(s_done, 1)

            def slot(t, g, j):
                n = peer_x(t)
                s = j % VR
                pe.wait_ge(diag_ready, g * TOPK + j + 1)
                pe.wait_ge(v_landed[s], (g * (TOPK // VR) + j // VR + 1) * 16)
                for c in range(2):
                    mm = pe.matmul(acc[0:n, c, :], diag[s][:, 0:n], v_ring[s][:, c * 512:(c + 1) * 512],
                                   start=False, stop=False, skip_group_check=True)
                mm.then_inc(v_free, 1)

            def step(t, g, nxt):
                for j in range(TOPK):
                    slot(t, g, j)
                    if g_is(g, 0) and j in (0, 2):
                        score_head(2 + j // 2)
                    if g_is(g, 1) and j % 2 == 0:
                        turn_xn(2 + j // 2)
                    for a, (tn, h, k) in zip(beside(g), nxt):
                        if isinstance(k, int) and k < HEADS and j == a:
                            pe.wait_ge(wq_in[h], 16)
                        if j == a:
                            queries(tn, h, k)
                        if j == a + 4:
                            turn_queries(tn, k)
                        if j == a + 8:
                            key_scores(tn, h, k)

            def score_head(k):
                pe.wait_ge(wq_in[k], 16)
                queries(0, k, k)
                turn_queries(0, k)
                if k == 0:
                    pe.wait_ge(keys_in, 16)
                key_scores(0, k, k)

            def start_sum(t):
                n = TILES[t][1]
                for c in range(2):
                    mm = pe.matmul(acc[0:n, c, :], ident[0:n, 0:n], x[0:n, t, c * 512:(c + 1) * 512],
                                   start=True, stop=False, skip_group_check=True)
                return mm

            pe.wait_ge(w_out_in, 16)
            pe.wait_ge(att_ready, len(ATT))
            pe.wait_ge(masked, len(ATT))
            project_out(0, 0)
            project_out(0, 1)
            project_out(1, 0)
            turn_xn(0)
            turn_xn(1)
            pe.wait_ge(xnT_ready, 2)
            score_head(0)
            score_head(1)
            for v in range(3, 2 * NT):
                project_out(v // 2, v % 2)
            pe.wait_ge(x2_ready, 2 * NT)
            start_sum(0)
            for t in range(NT):
                if t >= 1:
                    pe.wait_ge(acc_read, t)
                    start_sum(t)
                loop, rest = steps_of(t)
                if loop:
                    with pe.Fori(0, loop) as i:
                        step(t, i + FIRST[t], [(t + 1, i + 2, i + FIRST[t] + AHEAD + 1)])
                for g in rest:
                    step(t, g, scored_in(g))

        @block.scalar
        def _(act):
            def copy(out, src, scale=1.0):
                return nc.scalar.activation(out, src, ACT.Copy, scale=scale)

            ssq, rms = small[:, 0:8], small[:, 8:16]

            def root(t, summed, k, done):
                n = TILES[t][1]
                act.wait_ge(summed, k + 1)
                nc.scalar.activation(rms[0:n, t:t + 1], ssq[0:n, t:t + 1], ACT.Sqrt, scale=1.0 / D,
                                     bias=eps[0:n, :]).then_inc(done, 1)

            def square(t):
                n = TILES[t][1]
                act.wait_ge(x_in[t], 16)
                if t >= 2:
                    act.wait_ge(h_turned, t - 1)
                nc.scalar.activation(h_stage[t % 2][0:n, :], x[0:n, t, :], ACT.Square,
                                     accum_out=ssq[0:n, t:t + 1]).then_inc(summed, 1)
                root(t, summed, t, squared)

            def copy_turned(t):
                a, n = TILES[t]
                act.wait_ge(h_turned, t + 1)
                for c in range(2):
                    src = bank[2 + t % 2][:, c, :].rearrange("p (k n) -> p k n", k=4)[:, :, 0:n]
                    ins = copy(featT[:, 4 * c:4 * c + 4, a:a + n], src)
                ins.then_inc(hT_ready, 1)

            act.wait_ge(eps_set, 1)
            for t in range(NT + 1):
                if t < NT:
                    square(t)
                if t >= 1:
                    copy_turned(t - 1)

            def copy_qkT(i):
                c, t = QK[i]
                a, n = TILES[t]
                act.wait_ge(qk_turned, i + 1)
                dst = qT if CHUNKS[c][0] == "q" else kT
                b = (c - 1) % 2 * 3
                src = half(4 + i % 2)[:, 0:3 * P].rearrange("p (k n) -> p k n", k=3)[:, :, 0:n]
                copy(dst[:, b:b + 3, a:a + n], src).then_inc(qkT_ready, 1)

            for u, (c, t) in enumerate(UNITS):
                kind = CHUNKS[c][0]
                n = TILES[t][1]
                if kind == "uv":
                    st = lnst[0:n, 8 * t:8 * t + 8]
                    act.wait_ge(ln_stats, t + 1)
                    nc.scalar.activation(st[:, 5:6], st[:, 7:8], ACT.Sqrt, bias=eps[0:n, :]).then_inc(ln_root, 1)
                else:
                    act.wait_ge(proj_done, u + 1)
                    if kind == "v":
                        dst = v_tok[0:n, t, (c - 5) * HALF:(c - 4) * HALF]
                    else:
                        i = qk_at[c, t]
                        if kind == "q" and i >= 3:
                            act.wait_ge(qk_turned, i - 2)
                        dst = (q_stage[i % 3] if kind == "q" else k_stage[i - 2 * NT])[0:n, :]
                    scale = HD ** -0.5 if kind == "q" else 1.0
                    if grouped(c, t):
                        for g in range(NCG):
                            ins = copy(dst[:, g * P:(g + 1) * P], half(u % 3)[CG * g:CG * g + n, 0:P], scale)
                    else:
                        ins = copy(dst, half(u % 3)[0:n, 0:HALF], scale)
                    ins.then_inc(qkv_read, 1)
                if u >= 2 and UNITS[u - 2] in qk_at:
                    copy_qkT(qk_at[UNITS[u - 2]])

            for t, (a, n) in enumerate(TILES):
                act.wait_ge(g_turned, t + 1)
                src = half(6 + t % 2)[:, 0:2 * P].rearrange("p (k n) -> p k n", k=2)[:, :, 0:n]
                copy(featT[:, 0:2, a:a + n], src).then_inc(gT_ready, 1)

            def exps(u):
                r, n = span(ATT[u])
                act.wait_ge(masked, u + 1)
                st = att[:, 4 * (u % SR):4 * (u % SR) + 4]
                nc.scalar.activation(score[u % SR][0:r, 0:n], score[u % SR][0:r, 0:n], ACT.Exp, bias=st[0:r, 0:1],
                                     scale=-1.0, accum_out=st[0:r, 2:3]).then_inc(exped, 1)

            def copy_pT(u):
                r, n = span(ATT[u])
                act.wait_ge(p_turned, u + 1)
                if u >= 2:
                    act.wait_ge(pv_done, u - 1)
                if ATT[u][0] != "s":
                    copy(probT[u % 2][:, 0:n], half(4 + u % 2)[:, 0:n]).then_inc(pT_ready, 1)
                else:
                    m = CK // P * SROWS
                    copy(probT[u % 2][:, 0:m], half(4 + u % 2)[:, 0:m])
                    copy(probT[u % 2][0:NEWK, m:m + SROWS], half(4 + u % 2)[0:NEWK, m:m + SROWS]).then_inc(pT_ready, 1)

            for i in range(NG + 1):
                for u in group(i):
                    exps(u)
                for u in group(i - 1):
                    copy_pT(u)

            act.wait_ge(pv_done, len(ATT))
            act.wait_ge(v_out, 16 * (NT + 1))
            def copy_xnT(v):
                a, n = TILES[v // 2]
                act.wait_ge(xn_turned, v + 1)
                c = v % 2 * 4
                src = half(7).rearrange("p (k n) -> p k n", k=4)[:, :, 0:n]
                copy(featT[:, c:c + 4, a:a + n], src).then_inc(xnT_ready, 1)

            def square_x2(t):
                n = TILES[t][1]
                act.wait_ge(x2_ready, 2 * t + 2)
                nc.scalar.activation(xn[0:n, t, :], x[0:n, t, :], ACT.Square,
                                     accum_out=ssq[0:n, t:t + 1]).then_inc(summed, 1)
                root(t, summed, NT + t, squared2)

            def copy_q(t, k):
                n = TILES[t][1]
                act.wait_ge(q_done, k + 1)
                if not isinstance(k, int) or k:
                    act.wait_ge(q_turned, k)
                copy(q_row[0:n, :], ps_q[0:n, 0:2 * P]).then_inc(q_copied, 1)

            def copy_qT(t, k):
                n = TILES[t][1]
                act.wait_ge(q_turned, k + 1)
                if not isinstance(k, int) or k:
                    act.wait_ge(s_done, k)
                copy(q_col[:, :, 0:n], ps_qT[:, 0:2 * P].rearrange("p (c n) -> p c n", c=2)[:, :, 0:n]).then_inc(qT_copied, 1)

            def copy_s(t, k):
                n = TILES[t][1]
                act.wait_ge(s_done, k + 1)
                if not isinstance(k, int) or k > 2 * HEADS:
                    act.wait_ge(route_link, (k - 1) * LINKS + 2)
                elif k >= 2:
                    act.wait_ge(route_link, (k - 2) * LINKS + 2)
                copy(s_cur[s_buf(k)][0:n], ps_s[0:n, 0:2 * NKEYS].rearrange("p (c n) -> p c n", c=2)).then_inc(s_ready, 1)

            def exp_tops(t, lo, hi):
                n = TILES[t][1]
                act.wait_ge(route_link, (t * HEADS + hi) * LINKS)
                nc.scalar.activation(tops[0:n, lo:hi], tops[0:n, lo:hi], ACT.Exp).then_inc(tops_exped, 1)

            def step(t, g, nxt):
                n = peer_x(t)
                act.wait_ge(u_free, UR + (g + 1) * TOPK)
                nc.scalar.activation(gelu[:], hid[:], ACT.Gelu).then_inc(gelu_done, 1)
                if g_is(g, 0):
                    square_x2(SAMP)
                act.wait_ge(w_ready, g + 1)
                for j in range(TOPK):
                    act.wait_ge(v_free, g * TOPK + j + 1)
                    eye = ident if t < SAMP else ident4
                    nc.scalar.activation(diag[j % VR][:, 0:n], eye[:, 0:n], ACT.Copy,
                                         scale=wts[:, j:j + 1]).then_inc(diag_ready, 1)
                    if g_is(g, 0) and j in (2, 3):
                        copy_head(j)
                    if g_is(g, 1) and j % 2 == 1:
                        copy_xnT(2 + j // 2)
                    for a, (tn, _, k) in zip(beside(g), nxt):
                        if j == a + 4:
                            copy_q(tn, k)
                        if j == a + 8:
                            copy_qT(tn, k)
                        if j == a + 10:
                            copy_s(tn, k)

            def square_y(t):
                n = TILES[t][1]
                act.wait_ge(acc_read, t + 1)
                nc.scalar.activation(xn[0:n, t, :], x[0:n, t, :], ACT.Square,
                                     accum_out=ssq[0:n, t:t + 1]).then_inc(summed, 1)
                root(t, summed, 2 * NT + t, y_squared)

            def copy_head(k):
                copy_q(0, k)
                copy_qT(0, k)
                copy_s(0, k)

            square_x2(0)
            copy_xnT(0)
            copy_xnT(1)
            copy_head(0)
            copy_head(1)
            for t in range(1, NT - 1):
                square_x2(t)
            for t in range(NT):
                n = TILES[t][1]
                loop, rest = steps_of(t)
                if loop:
                    with act.Fori(0, loop) as i:
                        step(t, i + FIRST[t], [(t + 1, i + 2, i + FIRST[t] + AHEAD + 1)])
                for g in rest:
                    for heads in gates_in(g):
                        exp_tops(*heads)
                    step(t, g, scored_in(g))
                    if t >= 1 and g == rest[-2]:
                        square_y(t - 1)
                act.wait_ge(v_free, VR + (FIRST[t] + STEPS[t]) * TOPK)
                copy(x[0:n, t, :], acc[0:n].rearrange("p a b -> p (a b)")).then_inc(acc_read, 1)
            square_y(SAMP)

        @block.vector
        def _(dve):
            made_ops = [0]
            vec = nc.vector

            def then(ins):
                made_ops[0] += 1
                ins.then_inc(dv, 1)
                dve.wait_ge(dv, made_ops[0])

            rms, rstd = small[:, 8:16], small[:, 16:24]

            def scaled_norm(t, out, src):
                n = TILES[t][1]
                then(vec.reciprocal(rstd[0:n, t:t + 1], rms[0:n, t:t + 1]))
                return vec.scalar_tensor_tensor(out=out, in0=src, scalar=rstd[0:n, t:t + 1], in1=gain[0:n, :],
                                                op0=ALU.mult, op1=ALU.mult)

            vec.memset(eps[:], EPS).then_inc(eps_set, 1)
            dve.wait_ge(gain_in, 16)
            for t, (a, n) in enumerate(TILES):
                dve.wait_ge(squared, t + 1)
                scaled_norm(t, h_stage[t % 2][0:n, :], x[0:n, t, :]).then_inc(h_ready, 1)

            dve.wait_ge(consts_in, 16 * N_CONST)
            w3 = w_s[:].rearrange("p (g i) -> p g i", g=GA)
            vec.tensor_tensor(w3, w3, tril[:].unsqueeze(1).to_broadcast([P, GA, P]), ALU.mult)
            vec.tensor_tensor(
                w_sb[0:NSAMP, :].rearrange("p (g b i) -> p g b i", g=GA, b=NB),
                blockm[0:NSAMP, :].rearrange("p (o b i) -> p o b i", o=1, b=NB).to_broadcast([NSAMP, GA, NB, NS]),
                w_s32[0:NSAMP, :].rearrange("p (g o i) -> p g o i", g=GA, o=1).to_broadcast([NSAMP, GA, NB, NS]),
                ALU.mult).then_inc(ws_ready, 1)

            def split_uv(t, u):
                n = TILES[t][1]
                ps = half(u % 3)
                st = lnst[0:n, 8 * t:8 * t + 8]
                dve.wait_ge(proj_done, u + 1)
                vec.tensor_copy(u_tok[0:n, t, :], ps[0:n, 0:DA])
                v = vn[0:n, t, :]
                if t < SAMP:
                    raw = ps[0:n, DA:2 * DA]
                else:
                    then(vec.tensor_copy(v, ps[CG:CG + n, 0:DA]))
                    raw = v
                then(vec.bn_stats(st[:, 0:6], raw))
                vec.bn_aggr(st[:, 6:8], st[:, 0:6]).then_inc(ln_stats, 1)
                dve.wait_ge(ln_root, t + 1)
                then(vec.reciprocal(st[:, 7:8], st[:, 5:6]))
                ins = vec.tensor_scalar(v, raw, st[:, 6:7], st[:, 7:8], ALU.subtract, ALU.mult)
                ins.then_inc(uv_read, 1)
                dve.wait_ge(uv_read, t + 1)
                then(vec.tensor_tensor(v, v, lngb[0:n, 0, :], ALU.mult))
                then(vec.tensor_tensor(v, v, lngb[0:n, 1, :], ALU.add))

            def rotate(i, u):
                c, t = QK[i]
                n = TILES[t][1]
                nh = HALF // HD
                dve.wait_ge(qkv_read, u + 1 - NT)
                src = q_stage[i % 3] if CHUNKS[c][0] == "q" else k_stage[i - 2 * NT]
                xr = src[0:n, :].rearrange("p (h d) -> p h d", d=HD)
                ab = rope_ab[0:n, (i % 2) * 192:(i % 2) * 192 + 192].rearrange("p (a h d) -> p a h d", a=2, h=nh)
                cs = rope[0:n, 32 * t:32 * t + 32].rearrange("p (a o d) -> p a o d", a=4, o=1)
                vec.tensor_tensor(ab[:, 0], xr[:, :, 0:16],
                                  rope[0:n, 32 * t:32 * t + 16].unsqueeze(1).to_broadcast([n, nh, 16]), ALU.mult)
                vec.tensor_tensor(ab[:, 1, :, 0:8], xr[:, :, 8:16], cs[:, 2].to_broadcast([n, nh, 8]), ALU.mult)
                then(vec.tensor_tensor(ab[:, 1, :, 8:16], xr[:, :, 0:8], cs[:, 3].to_broadcast([n, nh, 8]), ALU.mult))
                vec.tensor_tensor(xr[:, :, 0:16], ab[:, 0], ab[:, 1], ALU.add).then_inc(roped, 1)

            def gate_u(t):
                n = TILES[t][1]
                dve.wait_ge(mixed_done, t + 1)
                b0 = 0 if t < SAMP else GA
                out = half(6 + t % 2)[0:n, 0:DA]
                ps = out.rearrange("p (g d) -> p g d", g=GA)
                then(vec.tensor_tensor(ps, ps, bs[0:n, b0:b0 + GA].unsqueeze(2).to_broadcast([n, GA, HD]), ALU.add))
                u3 = u_tok[0:n, t, :]
                vec.tensor_tensor(u3, u3, out, ALU.mult).then_inc(gated, 1)

            for u, (c, t) in enumerate(UNITS):
                if CHUNKS[c][0] == "uv":
                    split_uv(t, u)
                elif (c, t) in qk_at:
                    rotate(qk_at[c, t], u)
                if u in GMLP_AT:
                    gate_u(GMLP_AT.index(u))

            dve.wait_ge(k_out, 16 * 2 * NT)
            dve.wait_ge(qkT_ready, len(QK))

            def mask_max(u):
                unit = ATT[u]
                r, n = span(unit)
                st = att[:, 4 * (u % SR):4 * (u % SR) + 4]
                dve.wait_ge(scored, u + 1)
                if u >= SR:
                    dve.wait_ge(p_turned, u - SR + 1)

                def negated(out, scores, counts, least):
                    return vec.tensor_tensor_reduce(out=out, in0=scores, in1=counts, scale=-1.0, scalar=3e38,
                                                    op0=ALU.add, op1=ALU.min, accum_out=least)

                if unit[0] != "s":
                    negated(score[u % SR][:, 0:n], wide(u % 2, n), logc[:, 512 - n:512], st[:, 0:1]).then_inc(masked, 1)
                else:
                    b = unit[1]
                    negated(score[u % SR][0:r, 0:CK], wide(u % 2, CK)[0:r], smask[0:r, :], st[0:r, 1:2])
                    then(negated(score[u % SR][0:r, CK:n], wide(u % 2, n)[0:r, CK:n], snew[0:r, b, :], st[0:r, 3:4]))
                    vec.tensor_tensor(st[0:r, 0:1], st[0:r, 1:2], st[0:r, 3:4], ALU.min).then_inc(masked, 1)

            def normalise(u):
                r, n = span(ATT[u])
                st = att[:, 4 * (u % SR):4 * (u % SR) + 4]
                dve.wait_ge(exped, u + 1)
                then(vec.reciprocal(st[0:r, 3:4], st[0:r, 2:3]))
                vec.tensor_scalar(score[u % SR][0:r, 0:n], score[u % SR][0:r, 0:n], st[0:r, 3:4], None,
                                  ALU.mult).then_inc(normed, 1)

            def store_heads(u):
                unit = ATT[u]
                dve.wait_ge(pv_done, u + 1)
                out = half(6 + u % 2)
                if unit[0] != "s":
                    h, t = unit
                    r0 = HD * (h % 2)
                    vec.tensor_copy(featT[r0:r0 + HD, 2 + h // 2, t * P:(t + 1) * P],
                                    out[r0:r0 + HD, 0:P]).then_inc(att_ready, 1)
                else:
                    vec.tensor_copy(o_stage[0:OROWS, :], out[0:OROWS, 0:DB // NCG]).then_inc(o_copied, 1)

            def store_sample(u):
                b = ATT[u][1]
                dve.wait_ge(o_turned, b + 1)
                for g in range(NCG):
                    for s in range(2):
                        a = g * CG + s * NS
                        w = OROWS + 2 * NS
                        src = half(6 + u % 2)[HD * s:HD * s + HD, a:a + 2 * w].rearrange("p (r w) -> p r w", w=w)
                        ins = vec.tensor_copy(featT[HD * s:HD * s + HD, 2 + 2 * g:4 + 2 * g,
                                                    SEQ + NS * b:SEQ + NS * b + NS], src[:, :, 0:NS])
                ins.then_inc(att_ready, 1)

            for i in range(NG + 3):
                for u in group(i):
                    mask_max(u)
                for u in group(i - 3):
                    if ATT[u][0] == "s":
                        store_sample(u)
                for u in group(i):
                    normalise(u)
                for u in group(i - 2):
                    store_heads(u)

            dve.wait_ge(gain_in, 32)

            def norm_x2(t):
                n = TILES[t][1]
                dve.wait_ge(squared2, t + 1)
                scaled_norm(t, xn[0:n, t, :], x[0:n, t, :]).then_inc(xn_ready, 1)

            def add_x(t, c):
                n = TILES[t][1]
                if c == 0:
                    dve.wait_ge(x_in[t], 32)
                dve.wait_ge(out_done, 2 * t + c + 1)
                xh = x[0:n, t, c * 512:(c + 1) * 512]
                if t < SAMP:
                    ins = vec.tensor_tensor(xh, xh, half(c)[0:n, :], ALU.add)
                else:
                    for g, (lo, hi) in enumerate(OUT_COLS):
                        ins = vec.tensor_copy(xh[:, lo:hi], half(c)[CG * g:CG * g + n, 0:hi - lo])
                ins.then_inc(x2_ready, 1)

            def route(t, h, k, link):
                n = TILES[t][1]
                sc = [s_cur[s_buf(k)][0:n, c, :] for c in range(2)]
                sl = [s_left[0:n, c, :] for c in range(2)]
                wait_apart(dve, s_ready, k + 1)
                for c in range(2):
                    ins = vec.max(val[c][0:n, 0:8], sc[c])
                link(ins)
                for c in range(2):
                    vec.max_index(idx[c][0:n, 0:8], val[c][0:n, 0:8], sc[c])
                    ins = vec.match_replace(sl[c], val[c][0:n, 0:8], sc[c], -3e38)
                link(ins)
                for c in range(2):
                    ins = vec.max(val[c][0:n, 8:16], sl[c])
                link(ins)
                vec.tensor_tensor(cand[0:n, :].rearrange("p (i j) -> p i j", i=TOPK),
                                  val[0][0:n, :].unsqueeze(2).to_broadcast([n, TOPK, TOPK]),
                                  val[1][0:n, :].unsqueeze(1).to_broadcast([n, TOPK, TOPK]), ALU.add)
                for c in range(2):
                    ins = vec.max_index(idx[c][0:n, 8:16], val[c][0:n, 8:16], sl[c])
                link(ins)
                vec.max(top[0:n, 0:8], cand[0:n, :])
                for c in range(2):
                    ins = vec.tensor_copy(idf[c][0:n, :], idx[c][0:n, :])
                link(ins)
                vec.max_index(pos[0:n, 0:8], top[0:n, 0:8], cand[0:n, :])
                ins = vec.match_replace(cand_left[0:n, :], top[0:n, 0:8], cand[0:n, :], -3e38)
                link(ins)
                ins = vec.max(top[0:n, 8:16], cand_left[0:n, :])
                link(ins)
                vec.max_index(pos[0:n, 8:16], top[0:n, 8:16], cand_left[0:n, :])
                ins = vec.tensor_scalar(tops[0:n, bass.ds(h, 1), :].rearrange("p o k -> p (o k)"), top[0:n, :], top[0:n, 0:1],
                                  None, ALU.subtract)
                link(ins)
                vec.tensor_scalar(digit[0][0:n, :], pos[0:n, :], 4, None, ALU.logical_shift_right)
                ins = vec.tensor_scalar(digit[1][0:n, :], pos[0:n, :], TOPK - 1, None, ALU.bitwise_and)
                link(ins)
                for c in range(2):
                    ins = vec.tensor_tensor(hot[c][0:n], digit[c][0:n, :].unsqueeze(2).to_broadcast([n, TOPK, TOPK]),
                                      iota[0:n, :].unsqueeze(1).to_broadcast([n, TOPK, TOPK]), ALU.is_equal)
                link(ins)
                for c in range(2):
                    ins = vec.tensor_tensor(hot[c][0:n], hot[c][0:n], idf[c][0:n, :].unsqueeze(1).to_broadcast([n, TOPK, TOPK]),
                                      ALU.mult)
                link(ins)
                for c in range(2):
                    ins = vec.tensor_reduce(pick[c][0:n, :], hot[c][0:n], AX.X, ALU.add)
                link(ins)
                ins = vec.tensor_scalar(eidf[0:n, :], pick[0][0:n, :], float(NKEYS), None, ALU.mult)
                link(ins)
                dst = (eid[0:n, bass.ds(k * TOPK, TOPK)] if t < SAMP
                       else eid_samp[0:n, bass.ds(h * TOPK, TOPK)])
                vec.tensor_tensor(dst, eidf[0:n, :], pick[1][0:n, :], ALU.add).then_inc(
                    eid_ready if t < SAMP else eid_samp_ready, 1)

            def linker(start):
                done = [0]

                def link(ins):
                    done[0] += 1
                    ins.then_inc(route_link, 1)
                    wait_apart(dve, route_link, start + done[0])
                return link

            def finish_gates(t, lo, hi, n_exped):
                n = TILES[t][1]
                dve.wait_ge(tops_exped, n_exped)
                a, b = FIRST[t] + lo, FIRST[t] + hi
                g3 = (gate[0:n, a * TOPK:b * TOPK] if t < SAMP
                      else gate_samp[0:n, :]).rearrange("p (h k) -> p h k", h=hi - lo)
                then(vec.tensor_reduce(den8[0:n, lo:hi], tops[0:n, lo:hi], AX.X, ALU.add))
                then(vec.reciprocal(rden8[0:n, lo:hi], den8[0:n, lo:hi]))
                then(vec.tensor_tensor(g3, tops[0:n, lo:hi],
                                       rden8[0:n, lo:hi].unsqueeze(2).to_broadcast([n, hi - lo, TOPK]), ALU.mult))
                if t == SAMP:
                    to_groups(gate, gate_samp).then_inc(samp_gates, 1)
                    dve.wait_ge(samp_gates, 1)

            def to_groups(dst, src):
                a, m = FIRST[SAMP] * TOPK, SLOTS // GROUPS
                for g in range(GROUPS):
                    ins = vec.tensor_copy(dst[g * NSAMP:(g + 1) * NSAMP, a:a + m], src[0:NSAMP, g * m:(g + 1) * m])
                return ins

            def finish_y(t):
                n = TILES[t][1]
                s = rstd[0:n, t:t + 1]
                dve.wait_ge(y_squared, t + 1)
                then(vec.reciprocal(s, rms[0:n, t:t + 1]))
                vec.scalar_tensor_tensor(out=x[0:n, t, :], in0=x[0:n, t, :], scalar=s, in1=gain[0:n, :],
                                         op0=ALU.mult, op1=ALU.mult).then_inc(y_ready, 1)

            def set_x(t):
                if t < SAMP:
                    ins = vec.tensor_copy(x_cur, xn[:, t, :])
                else:
                    for g in range(GROUPS):
                        ins = vec.tensor_copy(x_cur[g * NSAMP:(g + 1) * NSAMP, :], xn[0:NSAMP, t, :])
                return ins

            def dots(g, lo, hi):
                for j in range(lo, hi):
                    s = j % UR
                    dve.wait_ge(u_landed[s], (g * (TOPK // UR) + j // UR + 1) * 16)
                    vec.tensor_tensor_reduce(out=u_ring[s], in0=u_ring[s], in1=x_cur, scale=1.0, scalar=0.0,
                                             op0=ALU.mult, op1=ALU.add, accum_out=hid[:, j:j + 1]).then_inc(u_free, 1)

            def weights(g):
                dve.wait_ge(gelu_done, g + 1)
                vec.tensor_tensor(wts[:], gelu[:], gate[:, bass.ds(g * TOPK, TOPK)], ALU.mult).then_inc(w_ready, 1)

            BETWEEN = 5

            def route_heads(g, heads):
                for i, (tn, h, k) in enumerate(heads):
                    if i == 1:
                        dots(g + 1, 0, BETWEEN)
                    route(tn, h, k, linker(k * LINKS))

            def step(g, gates, heads, next_tile=None):
                before = isinstance(g, int) and 0 < g < HEADS and len(routed_in(g - 1)) == 2
                dots(g, BETWEEN if before else 0, TOPK)
                weights(g)
                if next_tile is not None:
                    then(set_x(next_tile))
                for made in gates:
                    finish_gates(*made, n_gates[g])
                route_heads(g, heads)

            n_gates = {g: sum(len(gates_in(i)) for i in range(g + 1)) for g in range(NSTEP)}
            add_x(0, 0)
            add_x(0, 1)
            norm_x2(0)
            dve.wait_ge(xn_ready, 1)
            set_x(0).then_inc(u_free, UR)
            dve.sem_inc(v_free, VR)
            add_x(1, 0)
            route(0, 0, 0, linker(0))
            add_x(1, 1)
            route(0, 1, 1, linker(LINKS))
            for i in range(4):
                add_x(2 + i // 2, i % 2)
                if i % 2 == 0:
                    norm_x2(1 + i // 2)
                dots(0, 4 * i, 4 * i + 4)
            finish_gates(*gates_in(0)[0], 1)
            weights(0)
            add_x(SAMP, 0)
            norm_x2(SAMP - 1)
            add_x(SAMP, 1)
            norm_x2(SAMP)
            route_heads(0, [(0, k, k) for k in routed_in(0)])
            for t in range(NT):
                loop, rest = steps_of(t)
                if loop:
                    with dve.Fori(0, loop) as i:
                        step(i + FIRST[t], [], [(t + 1, i + 1, i + FIRST[t] + AHEAD)])
                for g in rest:
                    if g == FIRST[SAMP] - 1:
                        dve.wait_ge(eid_samp_ready, HEADS)
                        to_groups(eid, eid_samp).then_inc(eid_ready, STEPS[SAMP])
                    if g > 0:
                        step(g, gates_in(g), [(k // HEADS, k % HEADS, k) for k in routed_in(g)],
                             t + 1 if g == rest[-1] and t < SAMP else None)
                if t == 1:
                    dve.wait_ge(gain_in, 48)
                if t >= 1:
                    finish_y(t - 1)
            finish_y(SAMP)

        @block.gpsimd
        def _(pool):
            nc.gpsimd.dma_start(lngb, ln_gb.rearrange("(o a) d -> o a d", o=1).broadcast_to([P, 2, DA])).then_inc(consts_in, 16)
            for t, (a, n) in enumerate(TILES):
                nc.gpsimd.dma_start(rope[0:n, 32 * t:32 * t + 32], rope_c[a:a + n, :]).then_inc(consts_in, 16)
            nc.gpsimd.dma_start(w_s[:].rearrange("p (g i) -> p g i", g=GA), w_sT.rearrange("g j i -> j g i")).then_inc(consts_in, 16)
            for b in range(NB):
                nc.gpsimd.dma_start(w_s32[b * NS:(b + 1) * NS, :].rearrange("p (g i) -> p g i", g=GA),
                             w_sT[:, 0:NS, 0:NS].rearrange("g j i -> j g i")).then_inc(consts_in, 16)
                nc.gpsimd.dma_start(bs[b * NS:(b + 1) * NS, GA:2 * GA], b_sT[0:NS, :]).then_inc(consts_in, 16)
            nc.gpsimd.dma_start(bs[:, 0:GA], b_sT).then_inc(consts_in, 16)
            nc.gpsimd.dma_start(tril[:], tril_c).then_inc(consts_in, 16)
            nc.gpsimd.dma_start(blockm[0:NSAMP, :], blockm_c).then_inc(consts_in, 16)
            nc.gpsimd.dma_start(iota[:], iota_c).then_inc(consts_in, 16)
            nc.gpsimd.dma_start(logc, logc_c).then_inc(consts_in, 16)
            nc.gpsimd.dma_start(smask[0:NCG * CG, :], smask_c).then_inc(consts_in, 16)
            nc.gpsimd.dma_start(snew[0:NCG * CG], snew_c).then_inc(consts_in, 16)
            for g in range(GROUPS):
                nc.gpsimd.dma_start(ident4[g * NSAMP:(g + 1) * NSAMP, :], ident_c[0:NSAMP, 0:NSAMP]).then_inc(consts_in, 16)
            pool.wait_ge(k_out, 16 * 2 * NT)
            pool.wait_ge(qkT_ready, len(QK))
            for s in range(2):
                nc.gpsimd.memset(q_blk[s], 0.0).then_inc(qz, 1)
            pool.wait_ge(qz, 2)
            for b in range(NB):
                if b >= 2:
                    pool.wait_ge(scored, samp_at[b - 2] + 1)
                for i in range(2):
                    for s in range(2):
                        c = i * 2 * NS + s * NS
                        dst = q_blk[b % 2].rearrange("p (r w) -> p r w", w=CG)[HD * s:HD * s + HD, i::2, c:c + NS]
                        ins = nc.gpsimd.tensor_copy(
                            dst, qT[HD * s:HD * s + HD, i::2, SEQ + NS * b:SEQ + NS * b + NS])
                ins.then_inc(qb_ready, 1)
                if b >= 2:
                    pool.wait_ge(pv_done, samp_at[b - 2] + 1)
                else:
                    pool.wait_ge(proj_done, len(UNITS))
                    pool.wait_ge(kc_in[b], 16)
                nc.gpsimd.dma_start(vc[b % 2], v_cache[b][0:CK, :].rearrange("(c p) n -> p c n", p=P)).then_inc(
                    vc_in[b % 2], 16)

            def gather(ring, indices, s, table, column, landed, n_staged):
                nc.gpsimd.tensor_copy(indices[:, s:s + 1], eid[:, bass.ds(column, 1)]).then_inc(staged, 1)
                wait_apart(pool, staged, n_staged)
                nc.gpsimd.indirect_dma_start(
                    out=ring[s], out_offset=None, in_=table,
                    in_offset=bass.IndirectOffsetOnAxis(ap=indices[:, s:s + 1], axis=0)).then_inc(landed[s], 16)

            pool.wait_ge(eid_ready, 1)
            for j in range(TOPK):
                pool.wait_ge(u_free, j + 1)
                gather(u_ring, u_idx, j % UR, u_tab, j, u_landed, j + 1)

            def step(g, more):
                if more:
                    wait_apart(pool, eid_ready, g + 2)
                for j in range(TOPK):
                    before = (g * 2 + 1) * TOPK + (2 * j if more else j)
                    if more:
                        wait_apart(pool, u_free, (g + 1) * TOPK + j + 1)
                        gather(u_ring, u_idx, j % UR, u_tab, (g + 1) * TOPK + j, u_landed, before + 1)
                    wait_apart(pool, v_free, g * TOPK + j + 1)
                    gather(v_ring, v_idx, j % VR, v_tab, g * TOPK + j, v_landed, before + (2 if more else 1))

            with pool.Fori(0, NSTEP - 1) as g:
                step(g, True)
            step(NSTEP - 1, False)


def counts_log(dist, reach):
    c = sum(((dist >= 0) & (dist <= w // d * d) & (dist % d == 0) & reach).astype(np.int64) for w, d in BRANCHES)
    return np.where(c > 0, np.log(np.maximum(c, 1)), NEG).astype(np.float32)


def shape_tables():
    r = np.arange(P)
    ident = np.eye(P, dtype=np.float32)
    logc = counts_log(r[:, None] - np.arange(512)[None, :] + 384, True)
    m = np.arange(STRIDED)
    first = 16 * (m // NS) + m % NS
    near = np.arange(PAST - NEAR, PAST)
    rest = np.setdiff1d(np.arange(PAST), np.concatenate([first, near]))
    order = np.concatenate([first, near, rest])
    q = np.tile(np.arange(NS), NCG * CG // NS)
    smask = counts_log(PAST + q[:, None] - order[None, :CK], True)
    new_b, new_j = np.arange(NEWK) // NS, np.arange(NEWK) % NS
    snew = np.stack([counts_log(q[:, None] - new_j[None, :], new_b[None, :] == b) for b in range(NB)], axis=1)
    pos = np.concatenate([np.arange(SEQ), PAST + np.tile(np.arange(NS), NB)]).astype(np.float32)
    rot = HD // 4
    inv = np.float32(500000.0) ** (-np.arange(0, rot, 2, dtype=np.float32) / np.float32(rot))
    ang = pos[:, None] * inv[None, :].astype(np.float32)
    c, s = np.cos(ang), np.sin(ang)
    rope = np.concatenate([c, c, -s, s], axis=1).astype(np.float32)
    iota = np.tile(np.arange(TOPK, dtype=np.float32), (P, 1))
    tril = (r[:, None] <= r[None, :]).astype(np.float32)
    b, i = np.arange(NSAMP) // NS, np.arange(NSAMP) % NS
    blockm = ((b[:, None] == b[None, :]) & (i[:, None] <= i[None, :])).astype(np.float32)
    return order, dict(ident_c=ident, logc_c=logc, smask_c=smask, snew_c=snew, rope_c=rope, iota_c=iota,
                       tril_c=tril, blockm_c=blockm)


def kernel(x_prompt, x_sample, cache_k_win, cache_v_win, attn_norm, w_in, ln_v_g, ln_v_b, w_s, b_s, w_out,
           ffn_norm, peer_w_q, peer_sub_keys, peer_u, peer_v, final_norm):
    import concourse.bacc as bacc
    from concourse.bass_utils import run_bass_kernel_spmd

    f = np.asarray
    order, tables = shape_tables()
    arrays = dict(
        x_p=f(x_prompt)[0], x_s=f(x_sample).reshape(NSAMP, D),
        k_cache=f(cache_k_win)[0].reshape(NB, PAST, DB)[:, order].transpose(0, 2, 1),
        v_cache=f(cache_v_win)[0].reshape(NB, PAST, DB)[:, order],
        gains=np.stack([f(attn_norm)[0], f(ffn_norm)[0], f(final_norm)]),
        w_in=f(w_in)[0], ln_gb=np.stack([f(ln_v_g)[0], f(ln_v_b)[0]]),
        w_sT=f(w_s)[0].transpose(0, 2, 1), b_sT=f(b_s)[0].T, w_out=f(w_out)[0], w_q=f(peer_w_q)[0],
        keysT=f(peer_sub_keys)[0].reshape(2 * HEADS * NKEYS, P).T, u_tab=f(peer_u)[0], v_tab=f(peer_v)[0],
        **tables)
    outs = dict(y_p=(SEQ, D), y_s=(NSAMP, D), k_p=(SEQ, DB), v_p=(SEQ, DB), k_s=(NSAMP, DB), v_s=(NSAMP, DB),
                gv_s=(NSAMP, DA))
    nc = bacc.Bacc("TRN2", target_bir_lowering=False, num_devices=1)
    aps, feeds = {}, {}
    for name, a in arrays.items():
        a = np.ascontiguousarray(a)
        feeds["in_" + name] = a
        aps[name] = nc.dram_tensor("in_" + name, a.shape, mybir.dt.from_np(a.dtype), kind="ExternalInput").ap()
    for name, shape in outs.items():
        aps[name] = nc.dram_tensor("out_" + name, shape, F32, kind="ExternalOutput").ap()
    build(nc, **aps)
    got = run_bass_kernel_spmd(nc, [feeds], core_ids=[0]).results[0]
    y_p, y_s, k_p, v_p, k_s, v_s, gv_s = (got["out_" + name] for name in outs)
    return (y_p.reshape(1, SEQ, D), y_s.reshape(NB, NS, D),
            k_p.reshape(1, 1, SEQ, NH, HD), v_p.reshape(1, 1, SEQ, NH, HD),
            k_s.reshape(1, NB, NS, NH, HD), v_s.reshape(1, NB, NS, NH, HD), gv_s.reshape(1, NB, NS, DA))
```
